# Optimizing a Trainium2 kernel written in Bass

```python
import jax, jax.numpy as jnp
from jax import lax
import numpy as np

D_MODEL = 2048
BATCH = 1
SEQ = 256
DEPTH = 1

HEAD_DIM = 128
MIX_WIDTH = D_MODEL
A_WIDTH = MIX_WIDTH // 2
B_WIDTH = MIX_WIDTH - A_WIDTH
A_HEADS = A_WIDTH // HEAD_DIM
B_SUB_DIM = HEAD_DIM // 2
B_HEADS = B_WIDTH // (2 * B_SUB_DIM)
B_VDIM = 2 * B_SUB_DIM
IN_WIDTH = 3 * A_WIDTH + 3 * B_WIDTH
D_FF = 5632
ROPE_THETA = 500000.0
ROPE_FRACTION = 4
DILATED_PATTERNS = ((128, 1), (512, 4), (2048, 16))
Q_BLOCK = 128
EPS = 1e-6

kernel_name = "hybrid_dilated_diff_macaron_block"

def rms_norm(x, g):
    x32 = x.astype(jnp.float32)
    y = x32 * lax.rsqrt(jnp.mean(x32 * x32, axis=-1, keepdims=True) + EPS)
    return (y * g.astype(jnp.float32)).astype(x.dtype)

def swiglu_ffn(x, g, w_in, w_out):
    h = rms_norm(x, g)
    gate, up = jnp.split(h @ w_in, 2, axis=-1)
    return (jax.nn.silu(gate) * up) @ w_out

def partial_rope(x):
    S, hd = x.shape[1], x.shape[-1]
    rd = hd // ROPE_FRACTION
    half = rd // 2
    inv = ROPE_THETA ** (-jnp.arange(0, rd, 2, dtype=jnp.float32) / rd)
    ang = jnp.arange(S, dtype=jnp.float32)[:, None] * inv[None, :]
    bshape = (S,) + (1,) * (x.ndim - 3) + (half,)
    cos = jnp.cos(ang).reshape(bshape).astype(x.dtype)
    sin = jnp.sin(ang).reshape(bshape).astype(x.dtype)
    x1, x2, xp = x[..., :half], x[..., half:rd], x[..., rd:]
    return jnp.concatenate([x1 * cos - x2 * sin, x2 * cos + x1 * sin, xp], axis=-1)

def dilated_offsets():
    offs = []
    for window, dil in DILATED_PATTERNS:
        half = window // (2 * dil)
        offs.append(dil * jnp.arange(-half, half + 1, dtype=jnp.int32))
    return offs

def dilated_mixture_attention(q, k, v):
    B, H, S, hd = q.shape
    scale = hd ** -0.5
    offsets = dilated_offsets()

    def block(i):
        start = i * Q_BLOCK
        qb = lax.dynamic_slice_in_dim(q, start, Q_BLOCK, axis=2)
        pos = start + jnp.arange(Q_BLOCK, dtype=jnp.int32)
        outs, lses = [], []
        for offs in offsets:
            kpos = pos[:, None] + offs[None, :]
            valid = (kpos >= 0) & (kpos < S)
            idx = jnp.clip(kpos, 0, S - 1)
            kg = k[:, :, idx]
            vg = v[:, :, idx]
            s = jnp.einsum('bhqd,bhqkd->bhqk', qb, kg).astype(jnp.float32) * scale
            s = jnp.where(valid[None, None], s, -jnp.inf)
            lse = jax.nn.logsumexp(s, axis=-1)
            p = jnp.exp(s - lse[..., None])
            outs.append(jnp.einsum('bhqk,bhqkd->bhqd', p.astype(v.dtype), vg))
            lses.append(lse)
        o = jnp.stack(outs, axis=3)
        w = jax.nn.softmax(jnp.stack(lses, axis=-1), axis=-1)
        return jnp.einsum('bhqg,bhqgd->bhqd', w.astype(v.dtype), o)

    out = lax.map(block, jnp.arange(S // Q_BLOCK))
    return out.transpose(1, 2, 0, 3, 4).reshape(B, H, S, hd)

def differential_attention(q, k, v, lam):
    B, H, S = q.shape[:3]
    scale = q.shape[-1] ** -0.5

    def block(i):
        qb = lax.dynamic_slice_in_dim(q, i * Q_BLOCK, Q_BLOCK, axis=2)
        s = jnp.einsum('bhqcd,bhkcd->bhcqk', qb, k).astype(jnp.float32) * scale
        p = jax.nn.softmax(s, axis=-1)
        a = p[:, :, 0] - lam * p[:, :, 1]
        return jnp.einsum('bhqk,bhkd->bhqd', a.astype(v.dtype), v)

    out = lax.map(block, jnp.arange(S // Q_BLOCK))
    return out.transpose(1, 2, 0, 3, 4).reshape(B, H, S, v.shape[-1])

def hybrid_layer(x, layer_idx, ffn1_norm, ffn1_w_in, ffn1_w_out, mix_norm, w_in,
                 a_q_norm, a_k_norm, b_q_norm, b_k_norm,
                 lambda_q1, lambda_k1, lambda_q2, lambda_k2,
                 a_out_norm, b_out_norm, w_out, ffn2_norm, ffn2_w_in, ffn2_w_out):
    B, S, _ = x.shape
    x = x + 0.5 * swiglu_ffn(x, ffn1_norm, ffn1_w_in, ffn1_w_out)

    h = rms_norm(x, mix_norm)
    proj = h @ w_in
    a_q, a_k, a_v, b_q, b_k, b_v = jnp.split(
        proj, np.cumsum([A_WIDTH] * 3 + [B_WIDTH] * 2).tolist(), axis=-1)

    a_q = partial_rope(rms_norm(a_q.reshape(B, S, A_HEADS, HEAD_DIM), a_q_norm))
    a_k = partial_rope(rms_norm(a_k.reshape(B, S, A_HEADS, HEAD_DIM), a_k_norm))
    a_v = a_v.reshape(B, S, A_HEADS, HEAD_DIM)
    a_o = dilated_mixture_attention(a_q.transpose(0, 2, 1, 3), a_k.transpose(0, 2, 1, 3),
                                    a_v.transpose(0, 2, 1, 3))
    a_o = rms_norm(a_o, a_out_norm)

    b_q = partial_rope(rms_norm(b_q.reshape(B, S, B_HEADS, 2, B_SUB_DIM), b_q_norm))
    b_k = partial_rope(rms_norm(b_k.reshape(B, S, B_HEADS, 2, B_SUB_DIM), b_k_norm))
    b_v = b_v.reshape(B, S, B_HEADS, B_VDIM)
    lambda_init = 0.8 - 0.6 * float(np.exp(-0.3 * layer_idx))
    lam = (jnp.exp(jnp.sum(lambda_q1.astype(jnp.float32) * lambda_k1.astype(jnp.float32)))
           - jnp.exp(jnp.sum(lambda_q2.astype(jnp.float32) * lambda_k2.astype(jnp.float32)))
           + lambda_init)
    b_o = differential_attention(b_q.transpose(0, 2, 1, 3, 4), b_k.transpose(0, 2, 1, 3, 4),
                                 b_v.transpose(0, 2, 1, 3), lam)
    b_o = rms_norm(b_o, b_out_norm) * (1.0 - lambda_init)

    mixed = jnp.concatenate([a_o.transpose(0, 2, 1, 3).reshape(B, S, A_WIDTH),
                             b_o.transpose(0, 2, 1, 3).reshape(B, S, B_WIDTH)], axis=-1)
    x = x + mixed @ w_out

    x = x + 0.5 * swiglu_ffn(x, ffn2_norm, ffn2_w_in, ffn2_w_out)
    return x

def setup_inputs(seed: int = 0) -> dict:
    key = jax.random.key(seed)
    ks = jax.random.split(key, 20)
    f32 = jnp.float32

    def nrm(k, shape, scale):
        return jax.random.normal(k, shape, f32) * scale

    def gain(k, shape):
        return 1.0 + 0.02 * jax.random.normal(k, shape, f32)

    return {
        "x": jax.random.normal(ks[0], (BATCH, SEQ, D_MODEL), f32),
        "ffn1_norm": gain(ks[1], (DEPTH, D_MODEL)),
        "ffn1_w_in": nrm(ks[2], (DEPTH, D_MODEL, 2 * D_FF), D_MODEL ** -0.5),
        "ffn1_w_out": nrm(ks[3], (DEPTH, D_FF, D_MODEL), D_FF ** -0.5),
        "mix_norm": gain(ks[4], (DEPTH, D_MODEL)),
        "w_in": nrm(ks[5], (DEPTH, D_MODEL, IN_WIDTH), D_MODEL ** -0.5),
        "a_q_norm": gain(ks[6], (DEPTH, HEAD_DIM)),
        "a_k_norm": gain(ks[7], (DEPTH, HEAD_DIM)),
        "b_q_norm": gain(ks[8], (DEPTH, B_SUB_DIM)),
        "b_k_norm": gain(ks[9], (DEPTH, B_SUB_DIM)),
        "lambda_q1": nrm(ks[10], (DEPTH, B_SUB_DIM), 0.1),
        "lambda_k1": nrm(ks[11], (DEPTH, B_SUB_DIM), 0.1),
        "lambda_q2": nrm(ks[12], (DEPTH, B_SUB_DIM), 0.1),
        "lambda_k2": nrm(ks[13], (DEPTH, B_SUB_DIM), 0.1),
        "a_out_norm": gain(ks[14], (DEPTH, HEAD_DIM)),
        "b_out_norm": gain(ks[15], (DEPTH, B_VDIM)),
        "w_out": nrm(ks[16], (DEPTH, MIX_WIDTH, D_MODEL), MIX_WIDTH ** -0.5),
        "ffn2_norm": gain(ks[17], (DEPTH, D_MODEL)),
        "ffn2_w_in": nrm(ks[18], (DEPTH, D_MODEL, 2 * D_FF), D_MODEL ** -0.5),
        "ffn2_w_out": nrm(ks[19], (DEPTH, D_FF, D_MODEL), D_FF ** -0.5),
    }

def reference(x, ffn1_norm, ffn1_w_in, ffn1_w_out, mix_norm, w_in,
              a_q_norm, a_k_norm, b_q_norm, b_k_norm,
              lambda_q1, lambda_k1, lambda_q2, lambda_k2,
              a_out_norm, b_out_norm, w_out, ffn2_norm, ffn2_w_in, ffn2_w_out):
    for l in range(DEPTH):
        x = hybrid_layer(x, l, ffn1_norm[l], ffn1_w_in[l], ffn1_w_out[l], mix_norm[l], w_in[l],
                         a_q_norm[l], a_k_norm[l], b_q_norm[l], b_k_norm[l],
                         lambda_q1[l], lambda_k1[l], lambda_q2[l], lambda_k2[l],
                         a_out_norm[l], b_out_norm[l], w_out[l],
                         ffn2_norm[l], ffn2_w_in[l], ffn2_w_out[l])
    return x


_drawn_inputs = setup_inputs


def setup_inputs(seed=0):
    import zlib

    import numpy as np

    out = dict(_drawn_inputs(seed))
    spreads = {}
    factors = {'ffn1_norm': 4.724,
     'a_q_norm': 5.378,
     'a_k_norm': 5.477,
     'b_q_norm': 6.316,
     'b_k_norm': 5.483,
     'lambda_q1': 200.0,
     'a_out_norm': 99.676,
     'b_out_norm': 123.568,
     'ffn2_norm': 26.12,
     'lambda_q2': 59.568,
     'lambda_k2': 26.12}
    for name, (base, spread) in spreads.items():
        noise = np.random.default_rng([zlib.crc32(name.encode()), seed]).standard_normal(out[name].shape)
        drawn = base * np.exp(spread * noise) if base else spread * noise
        out[name] = __import__('jax').numpy.asarray(drawn.astype(out[name].dtype))
    for name, factor in factors.items():
        out[name] = (out[name] * factor).astype(out[name].dtype)
    return out
```

```python
from contextlib import ExitStack

import numpy as np

import concourse.bass as bass
from concourse import mybir

ALU = mybir.AluOpType
ACT = mybir.ActivationFunctionType
F32 = mybir.dt.float32
F32R = mybir.dt.float32r
I32 = mybir.dt.int32
AX_X = mybir.AxisListType.X

P = 128
SEQ = 256
TT = SEQ // P
D = 2048
FF = 5632
HD = 128
SUB = 64
NC = 512
KT = 4
KD = D // P
KF = FF // P
EPS = 1e-6
ROPE_THETA = 500000.0
PATTERNS = ((128, 1), (512, 4), (2048, 16))
SCALE_A = HD ** -0.5
SCALE_B = SUB ** -0.5
LAMBDA_INIT = 0.8 - 0.6 * float(np.exp(-0.3 * 0))
MASKED = -1e30
ROOT_MAGIC = 0x5F3759DF

RAW = 4
RING = 2
PARTS_D = [KT] * (KD // KT)
PARTS_F = [KT] * 8 + [3] * 4
assert sum(PARTS_F) == KF and len(PARTS_F) % RAW == 0

FFN_ITERS = FF // NC
HEADS_C = NC // HD
GROUPS = 4
UNITS = GROUPS * HEADS_C
SEG = 3 * len(PARTS_D)

N_IN, N_OUT, N_QKV, N_PROJ = FFN_ITERS * 8, 4 * len(PARTS_F), GROUPS * SEG, 4 * len(PARTS_D)
PIECE = np.cumsum([0, N_IN, N_OUT, N_QKV, N_PROJ, N_IN, N_OUT]).tolist()
CHUNK = np.cumsum([0, 2 * FFN_ITERS, 4, 3 * GROUPS, 4, 2 * FFN_ITERS, 4]).tolist()
IN1, OUT1, QKV, PROJ, IN2, OUT2 = range(6)
ROWS = np.cumsum([0, 4, FFN_ITERS, 4, 4, 4, FFN_ITERS]).tolist()
R_NORM1, R_FFN1, R_NORMX, R_MIX, R_NORM2, R_FFN2 = range(6)


def shape_constants():
    q, k = np.arange(SEQ)[:, None], np.arange(SEQ)[None, :]
    held = sum(((k - q) % d == 0) & (abs(k - q) <= w // 2) for w, d in PATTERNS)
    mask = np.where(held > 0, np.log(np.maximum(held, 1)) / SCALE_A, MASKED).astype(np.float32)
    parts = [np.eye(P, dtype=np.float32), mask.reshape(TT, P, SEQ).transpose(1, 0, 2).reshape(P, -1)]
    for width in (HD, SUB):
        rd = width // 4
        inv = (np.float32(ROPE_THETA) ** (-np.arange(0, rd, 2, dtype=np.float32) / np.float32(rd))).astype(np.float32)
        ang = np.arange(SEQ, dtype=np.float32)[:, None] * inv[None, :]
        for f in (np.cos, np.sin):
            parts.append(f(ang).astype(np.float32).reshape(TT, P, rd // 2).transpose(1, 0, 2).reshape(P, -1))
    return np.ascontiguousarray(np.concatenate(parts, axis=1))


N_CONST = P + TT * SEQ + 2 * TT * 16 + 2 * TT * 8


def hybrid_layer_kernel(nc, x, ffn1_norm, ffn1_w_in, ffn1_w_out, mix_norm, w_in, a_q_norm, a_k_norm, b_q_norm,
                        b_k_norm, lambda_q1, lambda_k1, lambda_q2, lambda_k2, a_out_norm, b_out_norm, w_out,
                        ffn2_norm, ffn2_w_in, ffn2_w_out, consts, out):
    x_dram = x[0].rearrange("(t p) d -> p t d", p=P)
    out_dram = out[0].rearrange("(t p) d -> p t d", p=P)

    def tiled(w):
        return w[0].rearrange("(c p) n -> p c n", p=P)

    with ExitStack() as ctx:
        def sb(name, shape, dt=F32, stack=ctx):
            return stack.enter_context(nc.sbuf_tensor(name, shape, dt))

        def sem(name):
            return ctx.enter_context(nc.semaphore(name))

        x_sb = sb("x_sb", [P, TT, D])
        rows = sb("rows", [P, 2, TT, NC])
        gain_row = sb("gain_row", [P, D])
        h_hi = sb("h_hi", [P, KD, SEQ], F32R)
        h_lo = sb("h_lo", [P, KD, SEQ], F32R)
        w_raw = sb("w_raw", [P, RAW, KT, NC])
        w_hi = sb("w_hi", [P, RING, KT, NC], F32R)
        w_lo = sb("w_lo", [P, RING, KT, NC], F32R)
        cst = sb("cst", [P, N_CONST])
        gains = sb("gains", [P, 4 * HD + 2 * SUB])
        sumsq = sb("sumsq", [P, TT, 4])
        rstd = sb("rstd", [P, TT])
        lam = sb("lam", [P, 4])
        root = sb("root", [P, 48])

        with ExitStack() as hidden:
            act_hi = sb("act_hi", [P, KF, SEQ], F32R, hidden)
            act_lo = sb("act_lo", [P, KF, SEQ], F32R, hidden)
        with ExitStack() as attention:
            mix_hi = sb("mix_hi", [P, KD, SEQ], F32R, attention)
            mix_lo = sb("mix_lo", [P, KD, SEQ], F32R, attention)
            qkv = sb("qkv", [P, 2, 3, TT, NC], F32, attention)
            squares = sb("squares", [P, TT, NC], F32, attention)
            rot = sb("rot", [P, 4, P], F32, attention)
            masked = sb("masked", [P, TT, SEQ], F32, attention)
            probs = sb("probs", [P, 2, TT, SEQ], F32, attention)
            weights = sb("weights", [P, TT, SEQ], F32, attention)
            qk_t = sb("qk_t", [P, 2, SEQ], F32, attention)
            w_t = sb("w_t", [P, TT, SEQ], F32, attention)
            head = sb("head", [P, TT, HD], F32, attention)
            head_sq = sb("head_sq", [P, TT, HD], F32, attention)
            head_ss = sb("head_ss", [P, TT], F32, attention)
            head_rstd = sb("head_rstd", [P, TT], F32, attention)
            qk_ss = sb("qk_ss", [P, TT * 8], F32, attention)
            qk_rstd = sb("qk_rstd", [P, TT * 8], F32, attention)
            row_max = sb("row_max", [P, 4], F32, attention)
            neg_max = sb("neg_max", [P, 4], F32, attention)
            row_sum = sb("row_sum", [P, 4], F32, attention)
            row_inv = sb("row_inv", [P, 2, 4], F32, attention)
            neg_lam_inv = sb("neg_lam_inv", [P, 2], F32, attention)

        acc = [ctx.enter_context(nc.psum_tensor(f"acc{i}", [P, TT, NC], F32)) for i in range(2)]
        turn = [ctx.enter_context(nc.psum_tensor(f"turn{i}", [P, TT * NC], F32)) for i in range(2)]
        turn4 = [t[:, :].rearrange("p (k s) -> p k s", s=SEQ) for t in turn]
        qk_turn = turn[0][:, 0:NC].rearrange("p (a s) -> p a s", s=SEQ)
        head_acc = turn[0][:, 0:TT * HD].rearrange("p (t d) -> p t d", d=HD)
        w_turn = turn[0][:, NC:2 * NC].rearrange("p (a s) -> p a s", s=SEQ)
        score = turn[1][:, :].rearrange("p (c t s) -> p c t s", t=TT, s=SEQ)

        ident = cst[:, 0:P]
        at = P
        mask = cst[:, at:at + TT * SEQ].rearrange("p (t s) -> p t s", t=TT)
        at += TT * SEQ
        rope = []
        for half in (16, 8):
            table = cst[:, at:at + 2 * TT * half].rearrange("p (f t r) -> p f t r", f=2, t=TT)
            rope.append((table[:, 0], table[:, 1]))
            at += 2 * TT * half
        g_aq, g_ak, g_ao, g_bo = (gains[:, HD * i:HD * (i + 1)] for i in range(4))
        g_bq, g_bk = (gains[:, 4 * HD + SUB * i:4 * HD + SUB * (i + 1)] for i in range(2))

        x_landed = sem("x_landed")
        const_landed = sem("const_landed")
        gain_landed = sem("gain_landed")
        raw_landed = [sem(f"raw_landed{i}") for i in range(RAW)]
        hi_ready = sem("hi_ready")
        lo_ready = sem("lo_ready")
        pieces_used = sem("pieces_used")
        bank_free = [sem(f"bank_free{i}") for i in range(2)]
        rows_ready = sem("rows_ready")
        rows_turned = sem("rows_turned")
        turn_hi = sem("turn_hi")
        turn_split = sem("turn_split")
        x_squared = sem("x_squared")
        dve_chain = sem("dve_chain")
        act_chain = sem("act_chain")
        lam_sums = sem("lam_sums")
        lam_exps = sem("lam_exps")
        lam_landed = sem("lam_landed")
        qk_squared = sem("qk_squared")
        qk_summed = sem("qk_summed")
        qk_normed = sem("qk_normed")
        qk_turned = sem("qk_turned")
        qk_t_ready = sem("qk_t_ready")
        scored = sem("scored")
        max_ready = sem("max_ready")
        probs_ready = sem("probs_ready")
        weights_ready = sem("weights_ready")
        w_turned = sem("w_turned")
        w_t_ready = sem("w_t_ready")
        head_done = sem("head_done")
        head_copied = sem("head_copied")
        head_written = sem("head_written")
        stored = sem("stored")

        def wait_chunk_read(eng, q):
            eng.wait_ge(bank_free[q % 2], q // 2 + 1)

        block = ctx.enter_context(nc.Block())

        @block.sync
        def _(sp):
            def load(src, slot, count, used):
                if used is not None:
                    sp.wait_ge(lo_ready, used)
                sp.dma_start(w_raw[:, slot, 0:count, :], src).then_inc(raw_landed[slot], 16)

            def load_chunk(stage, src, col, parts, first):
                k = 0
                for j, count in enumerate(parts):
                    known = isinstance(first, int)
                    used = None if known and first + j < RAW else first + j - RAW + 1
                    load(src[:, k:k + count, bass.ds(col, NC)], j % RAW, count, used)
                    k += count

            def ffn(w1, w2, s_in, s_out, gain, norms):
                gate_up = tiled(w1)
                with sp.Fori(1, FFN_ITERS) if s_in == IN1 else sp.Fori(0, FFN_ITERS) as i:
                    load_chunk(s_in, gate_up, i * NC, PARTS_D, i * 8 + PIECE[s_in])
                    load_chunk(s_in, gate_up, i * NC + FF, PARTS_D, i * 8 + PIECE[s_in] + 4)
                if gain is not None:
                    sp.wait_ge(rows_ready, norms)
                    sp.dma_start(gain_row[:, :], gain.to_broadcast([P, D])).then_inc(gain_landed, 16)
                down = tiled(w2)
                with sp.Fori(0, 4) as n:
                    load_chunk(s_out, down, n * NC, PARTS_F, n * len(PARTS_F) + PIECE[s_out])

            for t in range(TT):
                for n in range(2):
                    sp.dma_start(x_sb[:, t, n * 1024:(n + 1) * 1024],
                                 x_dram[:, t, n * 1024:(n + 1) * 1024]).then_inc(x_landed, 16)
            sp.dma_start(gain_row[:, :], ffn1_norm.to_broadcast([P, D])).then_inc(gain_landed, 16)
            gate_up1 = tiled(ffn1_w_in)
            load_chunk(IN1, gate_up1, 0, PARTS_D, 0)
            load_chunk(IN1, gate_up1, FF, PARTS_D, 4)
            ffn(ffn1_w_in, ffn1_w_out, IN1, OUT1, mix_norm, 4)
            qkv_w = tiled(w_in)
            for g in range(GROUPS):
                base = (g // 2) * 3 * (D // 2) + (g % 2) * NC
                for kind in range(3):
                    load_chunk(QKV, qkv_w, base + kind * (D // 2), PARTS_D, PIECE[QKV] + SEG * g + 4 * kind)
            sp.wait_ge(rows_ready, 8)
            sp.dma_start(gain_row[:, :], ffn2_norm.to_broadcast([P, D])).then_inc(gain_landed, 16)
            proj_w = tiled(w_out)
            with sp.Fori(0, 4) as n:
                load_chunk(PROJ, proj_w, n * NC, PARTS_D, n * 4 + PIECE[PROJ])
            ffn(ffn2_w_in, ffn2_w_out, IN2, OUT2, None, None)
            for c in range(4):
                wait_chunk_read(sp, CHUNK[OUT2] + c)
                sp.dma_start(out_dram[:, :, c * NC:(c + 1) * NC],
                             x_sb[:, :, c * NC:(c + 1) * NC]).then_inc(stored, 16)
            sp.wait_ge(stored, 64)

        @block.tensor
        def _(pe):
            def piece(p, j, k0, count, lhs, bank, first, last):
                pe.wait_ge(lo_ready, p + 1)
                slot = j % RING
                for kk in range(count):
                    for t in range(TT):
                        hi, lo = (a[:, k0 + kk, t * P:(t + 1) * P] for a in lhs)
                        o = acc[bank][:, t, :]
                        nc.tensor.matmul(o, hi, w_hi[:, slot, kk, :], start=first and kk == 0, stop=False)
                        nc.tensor.matmul(o, hi, w_lo[:, slot, kk, :], start=False, stop=False)
                        mm = nc.tensor.matmul(o, lo, w_hi[:, slot, kk, :], start=False,
                                              stop=last and kk == count - 1)
                mm.then_inc(pieces_used, 1)

            def bank_wait(bank, uses):
                pe.wait_ge(bank_free[bank], uses)

            def chunk(parts, p0, js, lhs, bank, r0=None):
                for j in js:
                    if r0 is not None:
                        pe.wait_ge(turn_split, r0 + j + 1)
                    k0 = sum(parts[:j])
                    piece(p0 + j, j, k0, parts[j], lhs, bank, j == 0, j == len(parts) - 1)

            def turn_rows(ready, count, buf, pair, held):
                pe.wait_ge(ready, count)
                if held is not None:
                    pe.wait_ge(turn_split, held)
                for k in range(4):
                    for t in range(TT):
                        mm = nc.tensor.transpose(turn4[pair][:, k, t * P:(t + 1) * P],
                                                 rows[:, buf, t, k * P:(k + 1) * P], ident)
                mm.then_inc(rows_turned, 1)

            def norm_turns(n, r0):
                for c in range(4):
                    turn_rows(rows_ready, 4 * n + c + 1, c % 2, c % 2, r0 + c - 1 if r0 + c > 1 else None)

            def ffn(s_in, s_out, r0):
                silu_up = bank_free[1]
                h, act = (h_hi, h_lo), (act_hi, act_lo)
                p0, uses = PIECE[s_in], CHUNK[s_in] // 2
                if uses:
                    bank_wait(0, uses)
                chunk(PARTS_D, p0, (0, 1), h, 0, r0 - 4)

                def gate_tail_and_up(i, wait_up=True, first=None):
                    chunk(PARTS_D, p0 + i * 8, (2, 3), h, 0, first)
                    if wait_up:
                        bank_wait(1, i + uses)
                    chunk(PARTS_D, p0 + i * 8 + 4, range(4), h, 1)

                def next_gate_and_turn(i):
                    bank_wait(0, i + uses + 1)
                    chunk(PARTS_D, p0 + i * 8 + 8, (0, 1), h, 0)
                    turn_rows(silu_up, i + uses + 1, 0, 0, i + r0)

                gate_tail_and_up(0, wait_up=uses > 0, first=r0 - 4)
                next_gate_and_turn(0)
                with pe.Fori(1, FFN_ITERS - 1) as i:
                    gate_tail_and_up(i)
                    next_gate_and_turn(i)
                gate_tail_and_up(FFN_ITERS - 1)
                turn_rows(silu_up, uses + FFN_ITERS, 0, 0, r0 + FFN_ITERS - 1)
                with pe.Fori(0, 2) as i:
                    for b in range(2):
                        bank_wait(b, i + CHUNK[s_out] // 2)
                        base = i * (2 * len(PARTS_F)) + PIECE[s_out] + b * len(PARTS_F)
                        chunk(PARTS_F, base, range(8), act, b)
                        pe.wait_ge(turn_split, r0 + FFN_ITERS)
                        chunk(PARTS_F, base, range(8, len(PARTS_F)), act, b)

            def turn_qk(u):
                g, h = divmod(u, HEADS_C)
                pe.wait_ge(qk_normed, 2 * g + 2)
                if u >= 2:
                    pe.wait_ge(head_copied, u - 1)
                for a in range(2):
                    for t in range(TT):
                        mm = nc.tensor.transpose(qk_turn[:, a, t * P:(t + 1) * P],
                                                 qkv[:, g % 2, a, t, h * HD:(h + 1) * HD], ident)
                mm.then_inc(qk_turned, 1)

            def scores(u):
                g = u // HEADS_C
                pe.wait_ge(qk_t_ready, u + 1)
                if u:
                    pe.wait_ge(probs_ready, u)
                subs = 1 if g < 2 else 2
                width = HD // subs
                for c in range(subs):
                    part = slice(c * width, (c + 1) * width)
                    for t in range(TT):
                        mm = nc.tensor.matmul(score[:, c, t, :], qk_t[part, 0, t * P:(t + 1) * P],
                                              qk_t[part, 1, :], start=True, stop=True)
                mm.then_inc(scored, 1)

            def turn_weights(u):
                pe.wait_ge(weights_ready, u + 1)
                src = probs[:, 0] if u // HEADS_C < 2 else weights
                for kt in range(TT):
                    for t in range(TT):
                        mm = nc.tensor.transpose(w_turn[:, kt, t * P:(t + 1) * P],
                                                 src[:, t, kt * P:(kt + 1) * P], ident)
                mm.then_inc(w_turned, 1)

            def values(u):
                g, h = divmod(u, HEADS_C)
                pe.wait_ge(w_t_ready, u + 1)
                wait_chunk_read(pe, CHUNK[QKV] + 3 * g + 2)
                if u + 1 < UNITS:
                    pe.wait_ge(qk_t_ready, u + 2)
                for t in range(TT):
                    for kt in range(TT):
                        mm = nc.tensor.matmul(head_acc[:, t, :], w_t[:, kt, t * P:(t + 1) * P],
                                              qkv[:, g % 2, 2, kt, h * HD:(h + 1) * HD],
                                              start=kt == 0, stop=kt == TT - 1)
                mm.then_inc(head_done, 1)

            def attention_step(s):
                u, phase = divmod(s, 3)
                if phase == 0:
                    if u % HEADS_C == 1 and u > 1:
                        pe.wait_ge(turn_split, ROWS[R_MIX] + u // HEADS_C)
                    if 1 <= u <= UNITS:
                        turn_weights(u - 1)
                    if u < UNITS:
                        turn_qk(u)
                if phase == 1:
                    if 1 <= u <= UNITS:
                        values(u - 1)
                    if u < UNITS:
                        scores(u)
                if phase == 2 and u and u % HEADS_C == 0:
                    g = u // HEADS_C - 1
                    pe.wait_ge(head_copied, u)
                    turn_rows(head_written, u, g % 2, 0, None)

            pe.wait_ge(const_landed, 16 * 7)
            norm_turns(0, ROWS[R_NORM1])
            ffn(IN1, OUT1, ROWS[R_FFN1])
            norm_turns(1, ROWS[R_NORMX])
            for g in range(GROUPS):
                for j in range(SEG):
                    q = CHUNK[QKV] + 3 * g + j // 4
                    if j % 4 == 0:
                        bank_wait(q % 2, q // 2)
                    chunk(PARTS_D, PIECE[QKV] + SEG * g + j - j % 4, (j % 4,), (h_hi, h_lo), q % 2,
                          ROWS[R_NORMX] if 3 * g + j < 4 else None)
                    if g:
                        attention_step(SEG * (g - 1) + j)
            for s in range(SEG * (GROUPS - 1), SEG * GROUPS + 3):
                attention_step(s)
            pe.wait_ge(turn_split, ROWS[R_MIX] + GROUPS)
            with pe.Fori(0, 2) as i:
                for b in range(2):
                    bank_wait(b, i + CHUNK[PROJ] // 2)
                    chunk(PARTS_D, i * 8 + PIECE[PROJ] + 4 * b, range(4), (mix_hi, mix_lo), b)
            norm_turns(2, ROWS[R_NORM2])
            ffn(IN2, OUT2, ROWS[R_FFN2])

        @block.scalar
        def _(act):
            chain = [0]

            def split_hi(p, quarter, j, count=KT, free=True):
                act.wait_ge(raw_landed[j % RAW], quarter * 16 + 16)
                if free:
                    act.wait_ge(pieces_used, p - RING + 1)
                nc.scalar.activation(w_hi[:, j % RING, 0:count, :], w_raw[:, j % RAW, 0:count, :],
                                     ACT.Copy).then_inc(hi_ready, 1)

            def turn_split_hi(r, dst, k, pair):
                act.wait_ge(rows_turned, r + 1)
                nc.scalar.activation(dst[:, bass.ds(k, 4), :], turn4[pair], ACT.Copy).then_inc(turn_hi, 1)

            def square_x(n, c):
                for t in range(TT):
                    before = 2 * (4 * n + c) + t
                    if before:
                        act.wait_ge(x_squared, before)
                    nc.scalar.activation(turn[1][:, t * NC:(t + 1) * NC], x_sb[:, t, c * NC:(c + 1) * NC],
                                         ACT.Square, accum_out=sumsq[:, t, c:c + 1]).then_inc(x_squared, 1)

            def norm_splits(r0):
                for c in range(4):
                    turn_split_hi(r0 + c, h_hi, 4 * c, c % 2)

            def pieces(stage, i, per, first, last, parts):
                for j in range(first, last):
                    p = i * per + PIECE[stage] + j
                    split_hi(p, i * (per // RAW) + (PIECE[stage] + j) // RAW, j, parts(j),
                             free=not isinstance(p, int) or p >= RING)

            full = lambda j: KT
            down = lambda j: PARTS_F[j % len(PARTS_F)]

            def silu(s_in, i, r0):
                act.wait_ge(pieces_used, i * 8 + PIECE[s_in] + 4)
                act.wait_ge(rows_turned, i + r0)
                nc.scalar.activation(rows[:, 0, :, :], acc[0][:, :, :], ACT.Silu).then_inc(bank_free[0], 1)

            def ffn(s_in, s_out, r0, final):
                pieces(s_in, 0, 8, 1, 3, full)
                def iteration(i):
                    pieces(s_in, i, 8, 3, 5, full)
                    silu(s_in, i, r0)
                    pieces(s_in, i, 8, 5, 11, full)
                    turn_split_hi(i + r0, act_hi, i * 4, 0)
                with act.Fori(0, FFN_ITERS - 1) as i:
                    iteration(i)
                i = FFN_ITERS - 1
                pieces(s_in, i, 8, 3, 5, full)
                silu(s_in, i, r0)
                pieces(s_in, i, 8, 5, 9, full)
                turn_split_hi(r0 + i, act_hi, i * 4, 0)
                n = 4 * len(PARTS_F)
                for c in range(4):
                    lo = c * len(PARTS_F)
                    pieces(s_out, 0, n, lo + 1, lo + 12, down)
                    if not (final and c == 3):
                        pieces(s_out, 0, n, lo + 12, lo + 13, down if c < 3 else full)
                    if not final:
                        wait_chunk_read(act, CHUNK[s_out] + c)
                        square_x(1, c)

            def copy_chunk(q):
                g, kind = divmod(q, 3)
                act.wait_ge(pieces_used, PIECE[QKV] + 4 * (q + 1))
                if g >= 2:
                    if kind < 2:
                        act.wait_ge(qk_turned, HEADS_C * (g - 1))
                    else:
                        act.wait_ge(head_done, HEADS_C * (g - 1))
                q_all = CHUNK[QKV] + q
                nc.scalar.activation(qkv[:, g % 2, kind, :, :], acc[q_all % 2][:, :, :],
                                     ACT.Copy).then_inc(bank_free[q_all % 2], 1)
                if kind < 2:
                    m = 2 * g + kind
                    if m:
                        act.wait_ge(qk_summed, m)
                    wait_chunk_read(act, q_all)
                    nc.scalar.activation(squares[:, :, :], qkv[:, g % 2, kind, :, :], ACT.Square).then_inc(qk_squared, 1)

            def copy_qk_t(u):
                act.wait_ge(qk_turned, u + 1)
                if u:
                    act.wait_ge(scored, u)
                nc.scalar.activation(qk_t[:, :, :], qk_turn, ACT.Copy).then_inc(qk_t_ready, 1)

            def exps(u):
                act.wait_ge(max_ready, u + 1)
                if u:
                    act.wait_ge(w_turned, u)
                    act.wait_ge(weights_ready, u)
                subs = 1 if u < UNITS // 2 else 2
                for c in range(subs):
                    for t in range(TT):
                        i = TT * c + t
                        src = masked[:, t, :] if subs == 1 else score[:, c, t, :]
                        s = nc.scalar.activation(probs[:, c, t, :], src, ACT.Exp, bias=neg_max[:, i:i + 1],
                                                 scale=SCALE_A if subs == 1 else SCALE_B,
                                                 accum_out=row_sum[:, i:i + 1])
                s.then_inc(probs_ready, 1)

            def copy_w_t(u):
                act.wait_ge(w_turned, u + 1)
                if u:
                    act.wait_ge(head_done, u)
                nc.scalar.activation(w_t[:, :, :], w_turn, ACT.Copy).then_inc(w_t_ready, 1)

            def copy_head(u):
                act.wait_ge(head_done, u + 1)
                if u:
                    act.wait_ge(head_written, u)
                for t in range(TT):
                    scale = row_inv[:, u % 2, t:t + 1] if u < UNITS // 2 else 1.0
                    s = nc.scalar.activation(head[:, t, :], head_acc[:, t, :], ACT.Copy, scale=scale)
                s.then_inc(act_chain, 1)
                chain[0] += 1
                act.wait_ge(act_chain, chain[0])
                for t in range(TT):
                    s = nc.scalar.activation(head_sq[:, t, :], head[:, t, :], ACT.Square,
                                             accum_out=head_ss[:, t:t + 1])
                s.then_inc(head_copied, 1)

            def attention_step(s):
                u, phase = divmod(s, 3)
                if phase == 0:
                    if u < UNITS:
                        copy_qk_t(u)
                    if 1 <= u <= UNITS:
                        copy_w_t(u - 1)
                if phase == 1:
                    if 1 <= u <= UNITS:
                        copy_head(u - 1)
                    if u < UNITS:
                        exps(u)
                if phase == 2 and u and u % HEADS_C == 0:
                    g = u // HEADS_C - 1
                    turn_split_hi(ROWS[R_MIX] + g, mix_hi, 4 * g, 0)

            act.dma_start(cst[:, :], consts).then_inc(const_landed, 16)
            for gain, dst in ((a_q_norm, g_aq), (a_k_norm, g_ak), (a_out_norm, g_ao), (b_out_norm, g_bo),
                              (b_q_norm, g_bq), (b_k_norm, g_bk)):
                act.dma_start(dst, gain.to_broadcast([P, gain.shape[1]])).then_inc(const_landed, 16)
            for n, vec in enumerate((lambda_q1, lambda_k1, lambda_q2, lambda_k2)):
                act.dma_start(rows[:, 1, 0, n * SUB:(n + 1) * SUB], vec.to_broadcast([P, SUB])).then_inc(lam_landed, 16)
            pieces(IN1, 0, 8, 0, 1, full)
            act.wait_ge(lam_sums, 1)
            nc.scalar.activation(lam[:, 2:4], lam[:, 0:2], ACT.Exp).then_inc(lam_exps, 1)
            act.wait_ge(x_landed, 64)
            for c in range(4):
                square_x(0, c)
            norm_splits(ROWS[R_NORM1])
            ffn(IN1, OUT1, ROWS[R_FFN1], False)
            norm_splits(ROWS[R_NORMX])
            for g in range(GROUPS):
                for j in range(SEG):
                    p = PIECE[QKV] + SEG * g + j + 1
                    split_hi(p, p // RAW, p)
                    if j % 4 == 0 and 3 * g + j // 4 > 0:
                        copy_chunk(3 * g + j // 4 - 1)
                    s = SEG * (g - 1) + j - 1
                    if s >= 0:
                        attention_step(s)
            copy_chunk(3 * GROUPS - 1)
            for s in range(SEG * (GROUPS - 1) - 1, SEG * GROUPS + 3):
                attention_step(s)
            for c in range(4):
                pieces(PROJ, 0, N_PROJ, 4 * c + 1, 4 * c + 5, full)
                wait_chunk_read(act, CHUNK[PROJ] + c)
                square_x(2, c)
            norm_splits(ROWS[R_NORM2])
            ffn(IN2, OUT2, ROWS[R_FFN2], True)

        @block.vector
        def _(dve):
            chain = [0]

            def link(ins):
                chain[0] += 1
                ins.then_inc(dve_chain, 1)
                dve.wait_ge(dve_chain, chain[0])

            def split_lo(p, j, count=KT):
                dve.wait_ge(hi_ready, p + 1)
                nc.vector.tensor_tensor(w_lo[:, j % RING, 0:count, :], w_raw[:, j % RAW, 0:count, :],
                                        w_hi[:, j % RING, 0:count, :].bitcast(F32),
                                        ALU.subtract).then_inc(lo_ready, 1)

            def turn_split_lo(r, dst_hi, dst_lo, k, pair):
                dve.wait_ge(turn_hi, r + 1)
                nc.vector.tensor_tensor(dst_lo[:, bass.ds(k, 4), :], turn4[pair],
                                        dst_hi[:, bass.ds(k, 4), :].bitcast(F32),
                                        ALU.subtract).then_inc(turn_split, 1)

            def inverse_root(y, src, width):
                n = y.shape[1]
                mean, square, bits = root[:, 0:n], root[:, 16:16 + n], root[:, 32:32 + n].bitcast(I32)
                link(nc.vector.tensor_scalar(mean, src, 1.0 / width, EPS, ALU.mult, ALU.add))
                link(nc.vector.tensor_scalar(bits, mean.bitcast(I32), 1, None, ALU.arith_shift_right))
                link(nc.vector.tensor_scalar(y.bitcast(I32), bits, -1, ROOT_MAGIC, ALU.mult, ALU.add))
                for _ in range(3):
                    link(nc.vector.tensor_tensor(square, y, y, ALU.mult))
                    link(nc.vector.scalar_tensor_tensor(square, square, -0.5, mean, ALU.mult, ALU.mult))
                    link(nc.vector.scalar_tensor_tensor(y, square, 1.5, y, ALU.add, ALU.mult))

            def norm(n, r0):
                dve.wait_ge(x_squared, 8 * (n + 1))
                link(nc.vector.tensor_reduce(rstd[:, :], sumsq[:, :, :], AX_X, ALU.add))
                inverse_root(rstd[:, :], rstd[:, :], D)
                dve.wait_ge(gain_landed, 16 * (n + 1))
                for c in range(5):
                    if c < 4:
                        if r0 + c > 1:
                            dve.wait_ge(rows_turned, r0 + c - 1)
                        for t in range(TT):
                            s = nc.vector.scalar_tensor_tensor(
                                rows[:, c % 2, t, :], x_sb[:, t, c * NC:(c + 1) * NC], rstd[:, t:t + 1],
                                gain_row[:, c * NC:(c + 1) * NC], ALU.mult, ALU.mult)
                        s.then_inc(rows_ready, 1)
                    if c:
                        turn_split_lo(r0 + c - 1, h_hi, h_lo, 4 * (c - 1), (c - 1) % 2)

            def product(s_in, i, r0):
                uses = CHUNK[s_in] // 2
                dve.wait_ge(bank_free[0], i + uses + 1)
                dve.wait_ge(pieces_used, i * 8 + PIECE[s_in] + 8)
                nc.vector.tensor_tensor(rows[:, 0, :, :], rows[:, 0, :, :], acc[1][:, :, :],
                                        ALU.mult).then_inc(bank_free[1], 1)

            def update_x(stage, c, per, weight):
                dve.wait_ge(pieces_used, PIECE[stage] + per * (c + 1))
                for t in range(TT):
                    o = x_sb[:, t, c * NC:(c + 1) * NC]
                    s = nc.vector.scalar_tensor_tensor(o, acc[c % 2][:, t, :], weight, o, ALU.mult, ALU.add)
                s.then_inc(bank_free[c % 2], 1)

            def pieces(stage, i, per, first, last, parts):
                for j in range(first, last):
                    split_lo(i * per + PIECE[stage] + j, j, parts(j))

            full = lambda j: KT
            down = lambda j: PARTS_F[j % len(PARTS_F)]

            def ffn(s_in, s_out, r0, final):
                pieces(s_in, 0, 8, 1, 3, full)
                with dve.Fori(0, FFN_ITERS - 1) as i:
                    pieces(s_in, i, 8, 3, 10, full)
                    product(s_in, i, r0)
                    pieces(s_in, i, 8, 10, 11, full)
                    turn_split_lo(i + r0, act_hi, act_lo, i * 4, 0)
                i = FFN_ITERS - 1
                pieces(s_in, i, 8, 3, 9, full)
                product(s_in, i, r0)
                turn_split_lo(i + r0, act_hi, act_lo, i * 4, 0)
                n = 4 * len(PARTS_F)
                for c in range(4):
                    lo = c * len(PARTS_F)
                    pieces(s_out, 0, n, lo + 1, lo + 12, down)
                    if not (final and c == 3):
                        pieces(s_out, 0, n, lo + 12, lo + 13, down if c < 3 else full)
                    update_x(s_out, c, len(PARTS_F), 0.5)

            def norm_qk(m, part):
                g, kind = divmod(m, 2)
                width = HD if g < 2 else SUB
                heads = NC // width
                gain = ((g_aq, g_ak), (g_bq, g_bk))[g // 2][kind]
                rows4 = qkv[:, g % 2, kind, :, :].rearrange("p t (h d) -> p t h d", d=width)
                shape = [P, TT, heads, width]
                ss, inv = qk_ss[:, 0:TT * heads], qk_rstd[:, 0:TT * heads]
                if part == 0:
                    dve.wait_ge(qk_squared, m + 1)
                    nc.vector.tensor_reduce(ss.rearrange("p (t h) -> p t h", t=TT), squares[:, :, :].rearrange("p t (h d) -> p t h d", d=width),
                                            AX_X, ALU.add).then_inc(qk_summed, 1)
                    dve.wait_ge(qk_summed, m + 1)
                    inverse_root(inv, ss, width)
                    for t in range(TT):
                        s = nc.vector.tensor_tensor(rows4[:, t], rows4[:, t],
                                                    inv[:, t * heads:(t + 1) * heads].unsqueeze(2).to_broadcast(shape[:1] + shape[2:]), ALU.mult)
                    link(s)
                    return
                for t in range(TT):
                    s = nc.vector.tensor_tensor(rows4[:, t], rows4[:, t],
                                                gain.unsqueeze(1).to_broadcast(shape[:1] + shape[2:]), ALU.mult)
                link(s)
                half = width // 8
                cos, sin = rope[g // 2]
                x1, x2 = rows4[:, :, :, 0:half], rows4[:, :, :, half:2 * half]
                temps = [rot[:, n, :].rearrange("p (t h r) -> p t h r", t=TT, h=heads) for n in range(4)]
                for n, (v, f) in enumerate(((x1, cos), (x2, sin), (x2, cos), (x1, sin))):
                    s = nc.vector.tensor_tensor(temps[n], v, f.unsqueeze(2).to_broadcast([P, TT, heads, half]), ALU.mult)
                link(s)
                nc.vector.tensor_tensor(x1, temps[0], temps[1], ALU.subtract)
                nc.vector.tensor_tensor(x2, temps[2], temps[3], ALU.add).then_inc(qk_normed, 1)

            def maxima(u):
                dve.wait_ge(scored, u + 1)
                if u:
                    dve.wait_ge(probs_ready, u)
                if u < UNITS // 2:
                    link(nc.vector.tensor_tensor(masked[:, :, :], score[:, 0], mask, ALU.add))
                    link(nc.vector.tensor_reduce(row_max[:, 0:TT], masked[:, :, :], AX_X, ALU.max))
                    nc.vector.tensor_scalar(neg_max[:, 0:TT], row_max[:, 0:TT], -SCALE_A, None,
                                            ALU.mult).then_inc(max_ready, 1)
                else:
                    link(nc.vector.tensor_reduce(row_max[:, :], score.rearrange("p c t s -> p (c t) s"), AX_X, ALU.max))
                    nc.vector.tensor_scalar(neg_max[:, :], row_max[:, :], -SCALE_B, None,
                                            ALU.mult).then_inc(max_ready, 1)

            def finish_weights(u):
                dve.wait_ge(probs_ready, u + 1)
                inv = row_inv[:, u % 2, :]
                if u < UNITS // 2:
                    nc.vector.reciprocal(inv[:, 0:TT], row_sum[:, 0:TT]).then_inc(weights_ready, 1)
                    return
                link(nc.vector.reciprocal(inv, row_sum[:, :]))
                link(nc.vector.tensor_scalar(neg_lam_inv[:, :], inv[:, TT:2 * TT], lam[:, 1:2], None, ALU.mult))
                for t in range(TT):
                    s = nc.vector.tensor_scalar(masked[:, t, :], probs[:, 1, t, :], neg_lam_inv[:, t:t + 1], None, ALU.mult)
                link(s)
                if u > UNITS // 2:
                    dve.wait_ge(w_turned, u)
                for t in range(TT):
                    s = nc.vector.scalar_tensor_tensor(weights[:, t, :], probs[:, 0, t, :], inv[:, t:t + 1],
                                                       masked[:, t, :], ALU.mult, ALU.add)
                s.then_inc(weights_ready, 1)

            def write_head(u):
                g, h = divmod(u, HEADS_C)
                dve.wait_ge(head_copied, u + 1)
                inverse_root(head_rstd[:, :], head_ss[:, :], HD)
                if h == 0:
                    r = ROWS[R_MIX] + g - 1
                    dve.wait_ge(rows_turned, r)
                for t in range(TT):
                    s = nc.vector.scalar_tensor_tensor(rows[:, g % 2, t, h * HD:(h + 1) * HD], head[:, t, :],
                                                       head_rstd[:, t:t + 1], g_ao if g < 2 else g_bo,
                                                       ALU.mult, ALU.mult)
                s.then_inc(head_written, 1)

            def attention_step(s):
                u, phase = divmod(s, 3)
                if phase == 1 and u < UNITS:
                    maxima(u)

            def attention_late(s):
                u, phase = divmod(s, 3)
                if phase == 1:
                    if 1 <= u <= UNITS:
                        write_head(u - 1)
                    if u < UNITS:
                        finish_weights(u)
                if phase == 2 and u and u % HEADS_C == 0:
                    g = u // HEADS_C - 1
                    turn_split_lo(ROWS[R_MIX] + g, mix_hi, mix_lo, 4 * g, 0)

            dve.wait_ge(const_landed, 16 * 7)
            dve.wait_ge(lam_landed, 16 * 4)
            lams = rows[:, 1, 0, 0:4 * SUB].rearrange("p (n d) -> p n d", n=4)
            for n in range(2):
                link(nc.vector.tensor_tensor(rows[:, 1, 1, n * SUB:(n + 1) * SUB], lams[:, 2 * n], lams[:, 2 * n + 1], ALU.mult))
            nc.vector.tensor_reduce(lam[:, 0:2], rows[:, 1, 1, 0:2 * SUB].rearrange("p (n d) -> p n d", n=2),
                                    AX_X, ALU.add).then_inc(lam_sums, 1)
            link(nc.vector.tensor_scalar(g_bo, g_bo, 1.0 - LAMBDA_INIT, None, ALU.mult))
            dve.wait_ge(lam_exps, 1)
            link(nc.vector.tensor_tensor(lam[:, 0:1], lam[:, 3:4], lam[:, 2:3], ALU.subtract))
            link(nc.vector.tensor_scalar(lam[:, 1:2], lam[:, 0:1], -LAMBDA_INIT, None, ALU.add))
            pieces(IN1, 0, 8, 0, 1, full)
            norm(0, ROWS[R_NORM1])
            ffn(IN1, OUT1, ROWS[R_FFN1], False)
            norm(1, ROWS[R_NORMX])
            for g in range(GROUPS):
                for j in range(SEG):
                    s = SEG * (g - 1) + j - 1
                    if s >= 0:
                        attention_step(s)
                    p = PIECE[QKV] + SEG * g + j + 1
                    split_lo(p, p)
                    if s >= 0:
                        attention_late(s)
                    if j in (5, 6, 9, 10):
                        norm_qk(2 * g + (j - 5) // 4, (j - 5) % 4)
            for s in range(SEG * (GROUPS - 1) - 1, SEG * GROUPS + 3):
                attention_step(s)
                attention_late(s)
            for c in range(4):
                pieces(PROJ, 0, N_PROJ, 4 * c + 1, 4 * c + 5, full)
                update_x(PROJ, c, 4, 1.0)
            norm(2, ROWS[R_NORM2])
            ffn(IN2, OUT2, ROWS[R_FFN2], True)


_INS = ["x", "ffn1_norm", "ffn1_w_in", "ffn1_w_out", "mix_norm", "w_in", "a_q_norm", "a_k_norm", "b_q_norm",
        "b_k_norm", "lambda_q1", "lambda_k1", "lambda_q2", "lambda_k2", "a_out_norm", "b_out_norm", "w_out",
        "ffn2_norm", "ffn2_w_in", "ffn2_w_out"]


def kernel(**inputs):
    import concourse.bacc as bacc
    from concourse.bass_utils import run_bass_kernel_spmd

    nc = bacc.Bacc("TRN2", target_bir_lowering=False, num_devices=1, dynamic_dma_scratch_size=1024)
    arrays = {f"in_{name}": np.ascontiguousarray(inputs[name]) for name in _INS}
    arrays["in_consts"] = shape_constants()
    args = [nc.dram_tensor(n, a.shape, mybir.dt.from_np(a.dtype), kind="ExternalInput").ap()
            for n, a in arrays.items()]
    out = nc.dram_tensor("out_y", (1, SEQ, D), F32, kind="ExternalOutput").ap()
    hybrid_layer_kernel(nc, *args, out)
    r = run_bass_kernel_spmd(nc, [arrays], core_ids=[0])
    return r.results[0]["out_y"]
```

```python
from contextlib import ExitStack

import numpy as np

import concourse.bass as bass
from concourse import mybir

ALU = mybir.AluOpType
ACT = mybir.ActivationFunctionType
F32 = mybir.dt.float32
F32R = mybir.dt.float32r
I32 = mybir.dt.int32
AX_X = mybir.AxisListType.X

P = 128
SEQ = 256
TT = SEQ // P
D = 2048
FF = 5632
HD = 128
SUB = 64
NC = 512
KT = 4
KD = D // P
KF = FF // P
EPS = 1e-6
ROPE_THETA = 500000.0
PATTERNS = ((128, 1), (512, 4), (2048, 16))
SCALE_A = HD ** -0.5
SCALE_B = SUB ** -0.5
LAMBDA_INIT = 0.8 - 0.6 * float(np.exp(-0.3 * 0))
MASKED = -1e30
ROOT_MAGIC = 0x5F3759DF

RAW = 4
RING = 4
UK = 2
PARTS_D = [KT] * (KD // KT)
PARTS_F = [KT] * 8 + [3] * 4
assert sum(PARTS_F) == KF and len(PARTS_F) % RAW == 0
UNITS_D, UNITS_F = 2 * len(PARTS_D), 2 * len(PARTS_F)

FFN_ITERS = FF // NC
HEADS_C = NC // HD
GROUPS = 4
HEADS = GROUPS * HEADS_C
SEG = 3 * len(PARTS_D)

N_IN, N_OUT, N_QKV, N_PROJ = FFN_ITERS * 8, 4 * len(PARTS_F), GROUPS * SEG, 4 * len(PARTS_D)
PROJ_ORDER = [(0, 0), (0, 1), (0, 2), (1, 0), (1, 1), (1, 2), (0, 3), (1, 3)] + [(c, j) for c in (2, 3) for j in range(4)]
PIECE = np.cumsum([0, N_IN, N_OUT, N_QKV, N_PROJ, N_IN, N_OUT]).tolist()
READS = np.cumsum([[0, 0], [FFN_ITERS, 0], [2, 2], [6, 6], [2, 2], [FFN_ITERS, 0], [2, 2]], axis=0).tolist()
IN1, OUT1, QKV, PROJ, IN2, OUT2 = range(6)
ROWS = np.cumsum([0, 4, FFN_ITERS, 4, 4, 4, FFN_ITERS]).tolist()
R_NORM1, R_FFN1, R_NORMX, R_MIX, R_NORM2, R_FFN2 = range(6)


XG_TURN = {17: 0, 19: 1, 27: 2}
XG_UPDATE = {17: 0, 19: 1, 27: 2, 35: 3}
XG_SQUARE = {18: 0, 20: 1, 29: 2}


def shape_constants():
    q, k = np.arange(SEQ)[:, None], np.arange(SEQ)[None, :]
    held = sum(((k - q) % d == 0) & (abs(k - q) <= w // 2) for w, d in PATTERNS)
    mask = np.where(held > 0, np.log(np.maximum(held, 1)) / SCALE_A, MASKED).astype(np.float32)
    parts = [np.eye(P, dtype=np.float32), mask.reshape(TT, P, SEQ).transpose(1, 0, 2).reshape(P, -1)]
    for width in (HD, SUB):
        rd = width // 4
        inv = (np.float32(ROPE_THETA) ** (-np.arange(0, rd, 2, dtype=np.float32) / np.float32(rd))).astype(np.float32)
        ang = np.arange(SEQ, dtype=np.float32)[:, None] * inv[None, :]
        for f in (np.cos, np.sin):
            parts.append(f(ang).astype(np.float32).reshape(TT, P, rd // 2).transpose(1, 0, 2).reshape(P, -1))
    return np.ascontiguousarray(np.concatenate(parts, axis=1))


N_CONST = P + TT * SEQ + 2 * TT * 16 + 2 * TT * 8


def hybrid_layer_kernel(nc, x, ffn1_norm, ffn1_w_in, ffn1_w_out, mix_norm, w_in, a_q_norm, a_k_norm, b_q_norm,
                        b_k_norm, lambda_q1, lambda_k1, lambda_q2, lambda_k2, a_out_norm, b_out_norm, w_out,
                        ffn2_norm, ffn2_w_in, ffn2_w_out, consts, out):
    x_dram = x[0].rearrange("(t p) d -> p t d", p=P)
    out_dram = out[0].rearrange("(t p) d -> p t d", p=P)

    def tiled(w):
        return w[0].rearrange("(c p) n -> p c n", p=P)

    with ExitStack() as ctx:
        def sb(name, shape, dt=F32, stack=ctx):
            return stack.enter_context(nc.sbuf_tensor(name, shape, dt))

        def sem(name):
            return ctx.enter_context(nc.semaphore(name))

        x_sb = sb("x_sb", [P, TT, D])
        rows = sb("rows", [P, 2, TT, NC])
        gain_row = sb("gain_row", [P, D])
        h_hi = sb("h_hi", [P, KD, SEQ], F32R)
        h_lo = sb("h_lo", [P, KD, SEQ], F32R)
        w_raw = sb("w_raw", [P, RAW, KT, NC])
        w_hi = sb("w_hi", [P, RING, UK, NC], F32R)
        w_lo = sb("w_lo", [P, RING, UK, NC], F32R)
        cst = sb("cst", [P, N_CONST])
        gains = sb("gains", [P, 4 * HD + 2 * SUB])
        dump = sb("dump", [P, NC], mybir.dt.bfloat16)
        sumsq = sb("sumsq", [P, TT, 4])
        rstd = sb("rstd", [P, TT])
        lam = sb("lam", [P, 4])
        root = sb("root", [P, 48])

        with ExitStack() as hidden:
            act_hi = sb("act_hi", [P, KF, SEQ], F32R, hidden)
            act_lo = sb("act_lo", [P, KF, SEQ], F32R, hidden)
        with ExitStack() as attention:
            mix_hi = sb("mix_hi", [P, KD, SEQ], F32R, attention)
            mix_lo = sb("mix_lo", [P, KD, SEQ], F32R, attention)
            qkv = sb("qkv", [P, 2, 3, TT, NC], F32, attention)
            squares = sb("squares", [P, TT, NC], F32, attention)
            rot = sb("rot", [P, 4, P], F32, attention)
            masked = sb("masked", [P, TT, SEQ], F32, attention)
            probs = sb("probs", [P, 2, TT, SEQ], F32, attention)
            weights = sb("weights", [P, TT, SEQ], F32, attention)
            qk_t = sb("qk_t", [P, 2, SEQ], F32, attention)
            w_t = sb("w_t", [P, TT, SEQ], F32, attention)
            head_sq = sb("head_sq", [P, TT, HD], F32, attention)
            head_ss = sb("head_ss", [P, TT * HEADS_C], F32, attention)
            head_rstd = sb("head_rstd", [P, TT * HEADS_C], F32, attention)
            lam_in = sb("lam_in", [P, 4, SUB], F32, attention)
            lam_prod = sb("lam_prod", [P, 2, SUB], F32, attention)
            qk_ss = sb("qk_ss", [P, TT * 8], F32, attention)
            qk_rstd = sb("qk_rstd", [P, TT * 8], F32, attention)
            row_max = sb("row_max", [P, 4], F32, attention)
            neg_max = sb("neg_max", [P, 4], F32, attention)
            row_sum = sb("row_sum", [P, 4], F32, attention)
            row_inv = sb("row_inv", [P, 2, 4], F32, attention)
            neg_lam_inv = sb("neg_lam_inv", [P, 2], F32, attention)

        acc = [ctx.enter_context(nc.psum_tensor(f"acc{i}", [P, TT, NC], F32)) for i in range(2)]
        turn = [ctx.enter_context(nc.psum_tensor(f"turn{i}", [P, TT * NC], F32)) for i in range(2)]
        turn4 = [t[:, :].rearrange("p (k s) -> p k s", s=SEQ) for t in turn]
        qk_turn = turn[0][:, 0:NC].rearrange("p (a s) -> p a s", s=SEQ)
        head_acc = turn[0][:, 0:TT * HD].rearrange("p (t d) -> p t d", d=HD)
        w_turn = turn[0][:, NC:2 * NC].rearrange("p (a s) -> p a s", s=SEQ)
        score = turn[1][:, :].rearrange("p (c t s) -> p c t s", t=TT, s=SEQ)

        ident = cst[:, 0:P]
        at = P
        mask = cst[:, at:at + TT * SEQ].rearrange("p (t s) -> p t s", t=TT)
        at += TT * SEQ
        rope = []
        for half in (16, 8):
            table = cst[:, at:at + 2 * TT * half].rearrange("p (f t r) -> p f t r", f=2, t=TT)
            rope.append((table[:, 0], table[:, 1]))
            at += 2 * TT * half
        g_aq, g_ak, g_ao, g_bo = (gains[:, HD * i:HD * (i + 1)] for i in range(4))
        g_bq, g_bk = (gains[:, 4 * HD + SUB * i:4 * HD + SUB * (i + 1)] for i in range(2))

        x_landed = [sem(f"x_landed{c}") for c in range(4)]
        ident_landed = sem("ident_landed")
        const_landed = sem("const_landed")
        gain_landed = sem("gain_landed")
        raw_landed = [sem(f"raw_landed{i}") for i in range(RAW)]
        hi_ready = sem("hi_ready")
        lo_ready = sem("lo_ready")
        units_used = sem("units_used")
        bank_free = [sem(f"bank_free{i}") for i in range(2)]
        rows_ready = sem("rows_ready")
        rows_turned = sem("rows_turned")
        turn_hi = sem("turn_hi")
        turn_split = sem("turn_split")
        x_squared = sem("x_squared")
        dve_chain = sem("dve_chain")
        pool_chain = sem("pool_chain")
        rstd_ready = sem("rstd_ready")
        lam_sums = sem("lam_sums")
        lam_exps = sem("lam_exps")
        qk_squared = sem("qk_squared")
        qk_summed = sem("qk_summed")
        qk_scaled = sem("qk_scaled")
        qk_normed = sem("qk_normed")
        qk_turned = sem("qk_turned")
        qk_t_ready = sem("qk_t_ready")
        scored = sem("scored")
        max_ready = sem("max_ready")
        probs_ready = sem("probs_ready")
        weights_ready = sem("weights_ready")
        w_turned = sem("w_turned")
        w_t_ready = sem("w_t_ready")
        head_done = sem("head_done")
        head_moved = sem("head_moved")
        head_copied = sem("head_copied")
        stored = sem("stored")

        def wait_read(eng, stage, q):
            eng.wait_ge(bank_free[q % 2], READS[stage][q % 2] + q // 2 + 1)

        def unit_k(parts, v):
            k0, count = sum(parts[:v // 2]), parts[v // 2]
            return (k0 + UK, count - UK) if v % 2 else (k0, UK)

        xg_at = [1, 0, 1, 0]

        block = ctx.enter_context(nc.Block())

        @block.sync
        def _(sp):
            def load(src, col, k0, count, p, j):
                if not isinstance(p, int) or p >= RAW:
                    sp.wait_ge(lo_ready, (p - RAW + 1) * 2)
                sp.dma_start(w_raw[:, j % RAW, 0:count, :],
                             src[:, k0:k0 + count, bass.ds(col, NC)]).then_inc(raw_landed[j % RAW], 16)

            def load_chunk(src, col, parts, p0):
                for j, count in enumerate(parts):
                    load(src, col, sum(parts[:j]), count, p0 + j, j)

            def ffn(w1, w2, s_in, s_out, started, gain, norms):
                gate_up = tiled(w1)
                with sp.Fori(started, FFN_ITERS) as i:
                    load_chunk(gate_up, i * NC, PARTS_D, i * 8 + PIECE[s_in])
                    load_chunk(gate_up, i * NC + FF, PARTS_D, i * 8 + PIECE[s_in] + 4)
                if gain is not None:
                    sp.wait_ge(rows_ready, norms)
                    sp.dma_start(gain_row[:, :], gain.to_broadcast([P, D])).then_inc(gain_landed, 16)
                down = tiled(w2)
                with sp.Fori(0, 4) as n:
                    load_chunk(down, n * NC, PARTS_F, n * len(PARTS_F) + PIECE[s_out])

            gate_up1 = tiled(ffn1_w_in)
            for c in range(4):
                cols = slice(c * NC, (c + 1) * NC)
                sp.dma_start(x_sb[:, :, cols], x_dram[:, :, cols]).then_inc(x_landed[c], 16)
                sp.dma_start(gain_row[:, cols], ffn1_norm[:, cols].to_broadcast([P, NC])).then_inc(x_landed[c], 16)
                load(gate_up1, 0, KT * c, KT, c, c)
            sp.dma_start(cst[:, P:N_CONST], consts[:, P:N_CONST]).then_inc(const_landed, 16)
            for gain, dst in ((a_q_norm, g_aq), (a_k_norm, g_ak), (a_out_norm, g_ao), (b_out_norm, g_bo),
                              (b_q_norm, g_bq), (b_k_norm, g_bk)):
                sp.dma_start(dst, gain.to_broadcast([P, gain.shape[1]])).then_inc(const_landed, 16)
            for n, vec in enumerate((lambda_q1, lambda_k1, lambda_q2, lambda_k2)):
                sp.dma_start(lam_in[:, n, :], vec.to_broadcast([P, SUB])).then_inc(const_landed, 16)
            load_chunk(gate_up1, FF, PARTS_D, 4)
            ffn(ffn1_w_in, ffn1_w_out, IN1, OUT1, 1, mix_norm, 4)
            qkv_w = tiled(w_in)
            for g in range(GROUPS):
                base = (g // 2) * 3 * (D // 2) + (g % 2) * NC
                for kind in range(3):
                    load_chunk(qkv_w, base + kind * (D // 2), PARTS_D, PIECE[QKV] + SEG * g + 4 * kind)
            sp.wait_ge(rows_ready, ROWS[R_MIX])
            sp.dma_start(gain_row[:, :], ffn2_norm.to_broadcast([P, D])).then_inc(gain_landed, 16)
            proj_w = tiled(w_out)
            for n, (c, j) in enumerate(PROJ_ORDER):
                load(proj_w, c * NC, j * KT, KT, PIECE[PROJ] + n, n)
            ffn(ffn2_w_in, ffn2_w_out, IN2, OUT2, 0, None, None)
            for c in range(4):
                wait_read(sp, OUT2, c)
                sp.dma_start(out_dram[:, :, c * NC:(c + 1) * NC],
                             x_sb[:, :, c * NC:(c + 1) * NC]).then_inc(stored, 16)
            sp.wait_ge(stored, 64)

        @block.tensor
        def _(pe):
            def unit(u, slot, k0, count, lhs, bank, first, last):
                pe.wait_ge(lo_ready, u + 1)
                for kk in range(count):
                    for t in range(TT):
                        hi, lo = (a[:, k0 + kk, t * P:(t + 1) * P] for a in lhs)
                        o = acc[bank][:, t, :]
                        nc.tensor.matmul(o, hi, w_hi[:, slot, kk, :], start=first and kk == 0, stop=False)
                        nc.tensor.matmul(o, hi, w_lo[:, slot, kk, :], start=False, stop=False)
                        mm = nc.tensor.matmul(o, lo, w_hi[:, slot, kk, :], start=False,
                                              stop=last and kk == count - 1)
                mm.then_inc(units_used, 1)

            def chunk(parts, u0, vs, lhs, bank, split=None):
                for v in vs:
                    if split is not None and v % 2 == 0:
                        pe.wait_ge(turn_split, split + v // 2 + 1)
                    k0, count = unit_k(parts, v)
                    unit(u0 + v, v % RING, k0, count, lhs, bank, v == 0, v == 2 * len(parts) - 1)

            def bank_wait(stage, b, uses):
                if not isinstance(uses, int) or READS[stage][b] + uses:
                    pe.wait_ge(bank_free[b], uses + READS[stage][b])

            def turn_rows(r, buf, split):
                pe.wait_ge(rows_ready, r + 1)
                if split is not None:
                    pe.wait_ge(turn_split, split)
                for k in range(4):
                    for t in range(TT):
                        mm = nc.tensor.transpose(turn4[buf][:, k, t * P:(t + 1) * P],
                                                 rows[:, buf, t, k * P:(k + 1) * P], ident)
                mm.then_inc(rows_turned, 1)

            h, act = (h_hi, h_lo), (act_hi, act_lo)

            def hidden(s_in, i, r0, first):
                u0 = i * 16 + 2 * PIECE[s_in]
                bank_wait(s_in, 0, i)
                chunk(PARTS_D, u0, range(4), h, 0, r0 - 4 if first else None)
                turn_rows(i + (r0 - 1), 0, i + (r0 - 1))
                chunk(PARTS_D, u0, range(4, 8), h, 0, r0 - 4 if first else None)
                if first:
                    bank_wait(s_in, 1, 0)
                else:
                    pe.wait_ge(rows_ready, i + r0)
                chunk(PARTS_D, u0 + 8, range(8), h, 1)

            def down(s_out, i, r0, turns):
                for b in range(2):
                    u0 = i * (2 * UNITS_F) + 2 * PIECE[s_out] + b * UNITS_F
                    bank_wait(s_out, b, i)
                    chunk(PARTS_F, u0, range(4), act, b)
                    if turns:
                        r = i * 2 + (r0 + FFN_ITERS - 1 + b)
                        turn_rows(r, b, r - b)
                    chunk(PARTS_F, u0, range(4, 20), act, b)
                    pe.wait_ge(turn_split, r0 + FFN_ITERS)
                    chunk(PARTS_F, u0, range(20, UNITS_F), act, b)

            def ffn(s_in, s_out, r0, final):
                hidden(s_in, 0, r0, True)
                with pe.Fori(1, FFN_ITERS) as i:
                    hidden(s_in, i, r0, False)
                pe.wait_ge(rows_ready, r0 + FFN_ITERS)
                if final:
                    turn_rows(r0 + FFN_ITERS - 1, 0, r0 + FFN_ITERS - 1)
                with pe.Fori(0, 2) as i:
                    down(s_out, i, r0, not final)

            def turn_qk(u):
                g, n = divmod(u, HEADS_C)
                pe.wait_ge(qk_normed, 2 * g + 2)
                if u >= 2:
                    pe.wait_ge(head_copied, u - 1)
                for a in range(2):
                    for t in range(TT):
                        mm = nc.tensor.transpose(qk_turn[:, a, t * P:(t + 1) * P],
                                                 qkv[:, g % 2, a, t, n * HD:(n + 1) * HD], ident)
                mm.then_inc(qk_turned, 1)

            def scores(u):
                pe.wait_ge(qk_t_ready, u + 1)
                if u:
                    pe.wait_ge(probs_ready, u)
                subs = 1 if u < HEADS // 2 else 2
                width = HD // subs
                for c in range(subs):
                    part = slice(c * width, (c + 1) * width)
                    for t in range(TT):
                        mm = nc.tensor.matmul(score[:, c, t, :], qk_t[part, 0, t * P:(t + 1) * P],
                                              qk_t[part, 1, :], start=True, stop=True)
                mm.then_inc(scored, 1)

            def turn_weights(u):
                pe.wait_ge(weights_ready, u + 1)
                src = probs[:, 0] if u < HEADS // 2 else weights
                for kt in range(TT):
                    for t in range(TT):
                        mm = nc.tensor.transpose(w_turn[:, kt, t * P:(t + 1) * P],
                                                 src[:, t, kt * P:(kt + 1) * P], ident)
                mm.then_inc(w_turned, 1)

            def values(u):
                g, n = divmod(u, HEADS_C)
                pe.wait_ge(w_t_ready, u + 1)
                wait_read(pe, QKV, 3 * g + 2)
                if u + 1 < HEADS:
                    pe.wait_ge(qk_t_ready, u + 2)
                for t in range(TT):
                    for kt in range(TT):
                        mm = nc.tensor.matmul(head_acc[:, t, :], w_t[:, kt, t * P:(t + 1) * P],
                                              qkv[:, g % 2, 2, kt, n * HD:(n + 1) * HD],
                                              start=kt == 0, stop=kt == TT - 1)
                mm.then_inc(head_done, 1)

            def attention_step(s):
                u, phase = divmod(s, 3)
                if phase == 0:
                    if u % HEADS_C == 1 and u > 1:
                        pe.wait_ge(turn_split, ROWS[R_MIX] + u // HEADS_C)
                    if 1 <= u <= HEADS:
                        turn_weights(u - 1)
                    if u < HEADS:
                        turn_qk(u)
                if phase == 1:
                    if 1 <= u <= HEADS:
                        values(u - 1)
                    if u < HEADS:
                        scores(u)
                if phase == 2 and u and u % HEADS_C == 0:
                    g = u // HEADS_C - 1
                    pe.wait_ge(head_copied, u)
                    pe.wait_ge(rows_ready, ROWS[R_MIX] + g + 1)
                    for k in range(4):
                        for t in range(TT):
                            mm = nc.tensor.transpose(turn4[0][:, k, t * P:(t + 1) * P],
                                                     rows[:, g % 2, t, k * P:(k + 1) * P], ident)
                    mm.then_inc(rows_turned, 1)

            def project(n):
                c, j = PROJ_ORDER[n // 2]
                v = 2 * j + n % 2
                if v == 0:
                    bank_wait(PROJ, c % 2, c // 2)
                if v % 2 == 0:
                    pe.wait_ge(turn_split, ROWS[R_MIX] + j + 1)
                k0, count = unit_k(PARTS_D, v)
                unit(2 * PIECE[PROJ] + n, n % RING, k0, count, (mix_hi, mix_lo), c % 2, v == 0, v == UNITS_D - 1)

            pe.wait_ge(ident_landed, 16)
            for c in range(4):
                r = ROWS[R_NORM1] + c
                if c < 3:
                    turn_rows(r, xg_at[c], r - 1 if c > 1 else None)
            ffn(IN1, OUT1, ROWS[R_FFN1], False)
            for g in range(GROUPS):
                for j in range(SEG):
                    q = 3 * g + j // 4
                    if j % 4 == 0:
                        bank_wait(QKV, q % 2, q // 2)
                    chunk(PARTS_D, 2 * PIECE[QKV] + 8 * q, range(2 * (j % 4), 2 * (j % 4) + 2), h, q % 2,
                          ROWS[R_NORMX] if q == 0 else None)
                    if g == 0 and j == 1:
                        turn_rows(ROWS[R_NORMX] + 3, xg_at[3], ROWS[R_NORMX] + 2)
                    if g:
                        attention_step(SEG * (g - 1) + j)
            for s in range(SEG * (GROUPS - 1), SEG * GROUPS + 3):
                if s < SEG * GROUPS:
                    project(s - SEG * (GROUPS - 1))
                attention_step(s)
            for n in range(SEG, 2 * len(PROJ_ORDER)):
                project(n)
                if n in XG_TURN:
                    c = XG_TURN[n]
                    turn_rows(ROWS[R_NORM2] + c, xg_at[c], ROWS[R_NORM2] + c - 1)
            ffn(IN2, OUT2, ROWS[R_FFN2], True)

        @block.scalar
        def _(act):
            def split_hi(stage, i, per, first, last, parts):
                for v in range(first, last):
                    u = i * (2 * per) + 2 * PIECE[stage] + v
                    count = unit_k(parts, v % (2 * len(parts)))[1]
                    act.wait_ge(raw_landed[v // 2 % RAW],
                                i * (per // RAW * 16) + (PIECE[stage] // RAW + v // 2 // RAW + 1) * 16)
                    if not isinstance(u, int) or u >= RING:
                        act.wait_ge(units_used, u - RING + 1)
                    k0 = v % 2 * UK
                    nc.scalar.activation(w_hi[:, v % RING, 0:count, :], w_raw[:, v // 2 % RAW, k0:k0 + count, :],
                                         ACT.Copy).then_inc(hi_ready, 1)

            def turn_split_hi(r, dst, k, pair):
                act.wait_ge(rows_turned, r + 1)
                nc.scalar.activation(dst[:, bass.ds(k, 4), :], turn4[pair], ACT.Copy).then_inc(turn_hi, 1)

            def square_x(n, c):
                for t in range(TT):
                    before = 2 * (4 * n + c) + t
                    if before:
                        act.wait_ge(x_squared, before)
                    nc.scalar.activation(dump[:, :], x_sb[:, t, c * NC:(c + 1) * NC],
                                         ACT.Square, accum_out=sumsq[:, t, c:c + 1]).then_inc(x_squared, 1)

            def silu(s_in, i):
                act.wait_ge(units_used, i * 16 + 2 * PIECE[s_in] + 8)
                for t in range(TT):
                    s = nc.scalar.activation(rows[:, 0, t, :], acc[0][:, t, :], ACT.Silu, scale=rstd[:, t:t + 1])
                s.then_inc(bank_free[0], 1)

            def ffn(s_in, s_out, r0, n, updated, final):
                split_hi(s_in, 0, 8, 4, 6, PARTS_D)
                updated()
                square_x(n, 3)
                split_hi(s_in, 0, 8, 6, 8, PARTS_D)
                turn_split_hi(r0 - 1, h_hi, 12, 0)
                split_hi(s_in, 0, 8, 8, 12, PARTS_D)
                act.wait_ge(rstd_ready, n + 1)
                silu(s_in, 0)
                split_hi(s_in, 0, 8, 12, 20, PARTS_D)
                with act.Fori(1, FFN_ITERS) as i:
                    split_hi(s_in, i, 8, 4, 8, PARTS_D)
                    turn_split_hi(i + (r0 - 1), act_hi, i * 4 - 4, 0)
                    split_hi(s_in, i, 8, 8, 12, PARTS_D)
                    silu(s_in, i)
                    split_hi(s_in, i, 8, 12, 20, PARTS_D)
                for c in range(4):
                    first = c * UNITS_F
                    split_hi(s_out, 0, 0, first + 4, first + 6, PARTS_F)
                    if c and not final:
                        wait_read(act, s_out, c - 1)
                        square_x(n + 1, c - 1)
                    split_hi(s_out, 0, 0, first + 6, first + 8, PARTS_F)
                    r = r0 + FFN_ITERS - 1 + c
                    if c == 0:
                        turn_split_hi(r, act_hi, KF - 4, 0)
                    elif not final:
                        turn_split_hi(r, h_hi, 4 * (c - 1), xg_at[c - 1])
                    last = first + UNITS_F if final and c == 3 else first + UNITS_F + 4
                    split_hi(s_out, 0, 0, first + 8, last, PARTS_F)

            def copy_chunk(q):
                g, kind = divmod(q, 3)
                act.wait_ge(units_used, 2 * PIECE[QKV] + UNITS_D * (q + 1))
                if g >= 2:
                    if kind < 2:
                        act.wait_ge(qk_turned, HEADS_C * (g - 1))
                    else:
                        act.wait_ge(head_done, HEADS_C * (g - 1))
                for t in range(TT):
                    s = nc.scalar.activation(qkv[:, g % 2, kind, t, :], acc[q % 2][:, t, :], ACT.Copy,
                                             scale=rstd[:, t:t + 1])
                s.then_inc(bank_free[q % 2], 1)
                if kind < 2:
                    m = 2 * g + kind
                    if m:
                        act.wait_ge(qk_summed, m)
                    wait_read(act, QKV, q)
                    nc.scalar.activation(squares[:, :, :], qkv[:, g % 2, kind, :, :], ACT.Square).then_inc(qk_squared, 1)

            def copy_qk_t(u):
                act.wait_ge(qk_turned, u + 1)
                if u:
                    act.wait_ge(scored, u)
                nc.scalar.activation(qk_t[:, :, :], qk_turn, ACT.Copy).then_inc(qk_t_ready, 1)

            def exps(u):
                act.wait_ge(max_ready, u + 1)
                if u:
                    act.wait_ge(w_turned, u)
                    act.wait_ge(weights_ready, u)
                subs = 1 if u < HEADS // 2 else 2
                for c in range(subs):
                    for t in range(TT):
                        i = TT * c + t
                        src = masked[:, t, :] if subs == 1 else score[:, c, t, :]
                        s = nc.scalar.activation(probs[:, c, t, :], src, ACT.Exp, bias=neg_max[:, i:i + 1],
                                                 scale=SCALE_A if subs == 1 else SCALE_B,
                                                 accum_out=row_sum[:, i:i + 1])
                s.then_inc(probs_ready, 1)

            def copy_w_t(u):
                act.wait_ge(w_turned, u + 1)
                if u:
                    act.wait_ge(head_done, u)
                nc.scalar.activation(w_t[:, :, :], w_turn, ACT.Copy).then_inc(w_t_ready, 1)

            def copy_head(u):
                g, n = divmod(u, HEADS_C)
                act.wait_ge(head_done, u + 1)
                if n == 0:
                    act.wait_ge(rows_turned, ROWS[R_MIX] + g)
                    act.wait_ge(rows_ready, ROWS[R_MIX] + g)
                if u:
                    act.wait_ge(head_copied, u)
                for t in range(TT):
                    scale = row_inv[:, u % 2, t:t + 1] if u < HEADS // 2 else 1.0
                    s = nc.scalar.activation(rows[:, g % 2, t, n * HD:(n + 1) * HD], head_acc[:, t, :], ACT.Copy,
                                             scale=scale)
                s.then_inc(head_moved, 1)
                act.wait_ge(head_moved, u + 1)
                for t in range(TT):
                    i = HEADS_C * t + n
                    s = nc.scalar.activation(head_sq[:, t, :], rows[:, g % 2, t, n * HD:(n + 1) * HD], ACT.Square,
                                             accum_out=head_ss[:, i:i + 1])
                s.then_inc(head_copied, 1)

            def attention_step(s):
                u, phase = divmod(s, 3)
                if phase == 0:
                    if u < HEADS:
                        copy_qk_t(u)
                    if 1 <= u <= HEADS:
                        copy_w_t(u - 1)
                if phase == 1:
                    if 1 <= u <= HEADS:
                        copy_head(u - 1)
                    if u < HEADS:
                        exps(u)
                if phase == 2 and u and u % HEADS_C == 0:
                    g = u // HEADS_C - 1
                    turn_split_hi(ROWS[R_MIX] + g, mix_hi, 4 * g, 0)

            act.dma_start(cst[:, 0:P], consts[:, 0:P]).then_inc(ident_landed, 16)
            for c in range(3):
                split_hi(IN1, 0, 8, c, c + 1, PARTS_D)
                turn_split_hi(ROWS[R_NORM1] + c, h_hi, 4 * c, xg_at[c])
                act.wait_ge(x_landed[c], 32)
                square_x(0, c)
            split_hi(IN1, 0, 8, 3, 4, PARTS_D)
            ffn(IN1, OUT1, ROWS[R_FFN1], 0, lambda: act.wait_ge(x_landed[3], 32), False)
            for g in range(GROUPS):
                for j in range(SEG):
                    if j % 4 == 0 and 3 * g + j // 4 > 0:
                        copy_chunk(3 * g + j // 4 - 1)
                    v = 2 * (SEG * g + j) + 4
                    split_hi(QKV, 0, 0, v, v + 1, PARTS_D)
                    s = SEG * (g - 1) + j - 1
                    if s >= 0:
                        attention_step(s)
                    split_hi(QKV, 0, 0, v + 1, v + 2, PARTS_D)
                    if g == 0 and j == 0:
                        wait_read(act, OUT1, 3)
                        square_x(1, 3)
                    if g == 0 and j == 1:
                        turn_split_hi(ROWS[R_NORMX] + 3, h_hi, 12, xg_at[3])
                        act.wait_ge(rstd_ready, 2)
                    if g == 0 and j == 2:
                        act.wait_ge(lam_sums, 1)
                        nc.scalar.activation(lam[:, 2:4], lam[:, 0:2], ACT.Exp).then_inc(lam_exps, 1)
            copy_chunk(3 * GROUPS - 1)
            for s in range(SEG * (GROUPS - 1) - 1, SEG * GROUPS + 3):
                attention_step(s)
                v = s - SEG * (GROUPS - 1) + 1 + 4
                if v < SEG + 4:
                    split_hi(PROJ, 0, 0, v, v + 1, PARTS_D)
            for v in range(SEG + 4, 2 * len(PROJ_ORDER) + 4):
                split_hi(PROJ, 0, 0, v, v + 1, PARTS_D)
                if v in XG_SQUARE:
                    wait_read(act, PROJ, XG_SQUARE[v])
                    square_x(2, XG_SQUARE[v])
                if v - 4 in XG_TURN:
                    c = XG_TURN[v - 4]
                    turn_split_hi(ROWS[R_NORM2] + c, h_hi, 4 * c, xg_at[c])
            ffn(IN2, OUT2, ROWS[R_FFN2], 2, lambda: wait_read(act, PROJ, 3), True)

        @block.vector
        def _(dve):
            chain = [0]

            def link(ins):
                chain[0] += 1
                ins.then_inc(dve_chain, 1)
                dve.wait_ge(dve_chain, chain[0])

            def split_lo(stage, i, per, first, last, parts):
                for v in range(first, last):
                    u = i * (2 * per) + 2 * PIECE[stage] + v
                    count = unit_k(parts, v % (2 * len(parts)))[1]
                    dve.wait_ge(hi_ready, u + 1)
                    k0 = v % 2 * UK
                    nc.vector.tensor_tensor(w_lo[:, v % RING, 0:count, :], w_raw[:, v // 2 % RAW, k0:k0 + count, :],
                                            w_hi[:, v % RING, 0:count, :].bitcast(F32),
                                            ALU.subtract).then_inc(lo_ready, 1)

            def turn_split_lo(r, dst_hi, dst_lo, k, pair):
                dve.wait_ge(turn_hi, r + 1)
                nc.vector.tensor_tensor(dst_lo[:, bass.ds(k, 4), :], turn4[pair],
                                        dst_hi[:, bass.ds(k, 4), :].bitcast(F32),
                                        ALU.subtract).then_inc(turn_split, 1)

            def inverse_root(y, src, width, done=None, count=0):
                n = y.shape[1]
                mean, square, bits = root[:, 0:n], root[:, 16:16 + n], root[:, 32:32 + n].bitcast(I32)
                link(nc.vector.tensor_scalar(mean, src, 1.0 / width, EPS, ALU.mult, ALU.add))
                link(nc.vector.tensor_scalar(bits, mean.bitcast(I32), 1, None, ALU.arith_shift_right))
                link(nc.vector.tensor_scalar(y.bitcast(I32), bits, -1, ROOT_MAGIC, ALU.mult, ALU.add))
                for step in range(3):
                    link(nc.vector.tensor_tensor(square, y, y, ALU.mult))
                    link(nc.vector.scalar_tensor_tensor(square, square, -0.5, mean, ALU.mult, ALU.mult))
                    last = nc.vector.scalar_tensor_tensor(y, square, 1.5, y, ALU.add, ALU.mult)
                    if step < 2 or done is None:
                        link(last)
                    else:
                        last.then_inc(done, 1)
                        dve.wait_ge(done, count)

            def norm_factor(n):
                dve.wait_ge(x_squared, 8 * (n + 1))
                link(nc.vector.tensor_reduce(rstd[:, :], sumsq[:, :, :], AX_X, ALU.add))
                inverse_root(rstd[:, :], rstd[:, :], D, rstd_ready, n + 1)

            def gain_x(r, c, turned):
                if turned:
                    dve.wait_ge(rows_turned, turned)
                cols = slice(c * NC, (c + 1) * NC)
                nc.vector.tensor_tensor(rows[:, xg_at[c], :, :], x_sb[:, :, cols],
                                        gain_row[:, cols].unsqueeze(1).to_broadcast([P, TT, NC]),
                                        ALU.mult).then_inc(rows_ready, 1)

            def product(s_in, i):
                dve.wait_ge(bank_free[0], i + READS[s_in][0] + 1)
                dve.wait_ge(units_used, i * 16 + 2 * PIECE[s_in] + 16)
                for t in range(TT):
                    s = nc.vector.scalar_tensor_tensor(rows[:, 0, t, :], acc[1][:, t, :], rstd[:, t:t + 1],
                                                       rows[:, 0, t, :], ALU.mult, ALU.mult)
                s.then_inc(rows_ready, 1)

            def update_x(stage, c, units, weight):
                dve.wait_ge(units_used, 2 * PIECE[stage] + units)
                for t in range(TT):
                    o = x_sb[:, t, c * NC:(c + 1) * NC]
                    s = nc.vector.scalar_tensor_tensor(o, acc[c % 2][:, t, :], weight, o, ALU.mult, ALU.add)
                s.then_inc(bank_free[c % 2], 1)
                wait_read(dve, stage, c)

            def ffn(s_in, s_out, r0, n, final):
                split_lo(s_in, 0, 8, 4, 8, PARTS_D)
                turn_split_lo(r0 - 1, h_hi, h_lo, 12, 0)
                norm_factor(n)
                split_lo(s_in, 0, 8, 8, 20, PARTS_D)
                if n == 0:
                    lambda_sums()
                product(s_in, 0)
                with dve.Fori(1, FFN_ITERS) as i:
                    split_lo(s_in, i, 8, 4, 8, PARTS_D)
                    turn_split_lo(i + (r0 - 1), act_hi, act_lo, i * 4 - 4, 0)
                    split_lo(s_in, i, 8, 8, 20, PARTS_D)
                    product(s_in, i)
                for c in range(4):
                    first = c * UNITS_F
                    split_lo(s_out, 0, 0, first + 4, first + 8, PARTS_F)
                    r = r0 + FFN_ITERS - 1 + c
                    if c == 0:
                        turn_split_lo(r, act_hi, act_lo, KF - 4, 0)
                    elif not final:
                        turn_split_lo(r, h_hi, h_lo, 4 * (c - 1), xg_at[c - 1])
                    last = first + UNITS_F if final and c == 3 else first + UNITS_F + 4
                    split_lo(s_out, 0, 0, first + 8, last, PARTS_F)
                    update_x(s_out, c, UNITS_F * (c + 1), 0.5)
                    if not final:
                        if c == 0:
                            dve.wait_ge(gain_landed, 16)
                        gain_x(r + 1, c, r)

            def lambda_sums():
                dve.wait_ge(const_landed, 16 * 11)
                pairs = lam_in[:, :, :].rearrange("p (n two) d -> p n two d", two=2)
                link(nc.vector.tensor_tensor(lam_prod[:, :, :], pairs[:, :, 0, :], pairs[:, :, 1, :], ALU.mult))
                nc.vector.tensor_reduce(lam[:, 0:2], lam_prod[:, :, :], AX_X, ALU.add).then_inc(lam_sums, 1)
                link(nc.vector.tensor_scalar(g_bo, g_bo, 1.0 - LAMBDA_INIT, None, ALU.mult))

            def negative_lambda():
                dve.wait_ge(lam_exps, 1)
                link(nc.vector.tensor_tensor(lam[:, 0:1], lam[:, 3:4], lam[:, 2:3], ALU.subtract))
                link(nc.vector.tensor_scalar(lam[:, 1:2], lam[:, 0:1], -LAMBDA_INIT, None, ALU.add))

            def scale_qk(m):
                g, kind = divmod(m, 2)
                width = HD if g < 2 else SUB
                heads = NC // width
                ss, inv = qk_ss[:, 0:TT * heads], qk_rstd[:, 0:TT * heads]
                dve.wait_ge(qk_squared, m + 1)
                nc.vector.tensor_reduce(ss.rearrange("p (t h) -> p t h", t=TT),
                                        squares[:, :, :].rearrange("p t (h d) -> p t h d", d=width),
                                        AX_X, ALU.add).then_inc(qk_summed, 1)
                dve.wait_ge(qk_summed, m + 1)
                inverse_root(inv, ss, width)
                for t in range(TT):
                    o = qkv[:, g % 2, kind, t, :].rearrange("p (h d) -> p h d", d=width)
                    s = nc.vector.tensor_tensor(o, o, inv[:, t * heads:(t + 1) * heads].unsqueeze(2)
                                                .to_broadcast([P, heads, width]), ALU.mult)
                s.then_inc(qk_scaled, 1)

            def maxima(u):
                dve.wait_ge(scored, u + 1)
                if u:
                    dve.wait_ge(probs_ready, u)
                if u < HEADS // 2:
                    link(nc.vector.tensor_tensor(masked[:, :, :], score[:, 0], mask, ALU.add))
                    link(nc.vector.tensor_reduce(row_max[:, 0:TT], masked[:, :, :], AX_X, ALU.max))
                    nc.vector.tensor_scalar(neg_max[:, 0:TT], row_max[:, 0:TT], -SCALE_A, None,
                                            ALU.mult).then_inc(max_ready, 1)
                else:
                    link(nc.vector.tensor_reduce(row_max[:, :], score.rearrange("p c t s -> p (c t) s"), AX_X, ALU.max))
                    nc.vector.tensor_scalar(neg_max[:, :], row_max[:, :], -SCALE_B, None,
                                            ALU.mult).then_inc(max_ready, 1)

            def finish_weights(u):
                dve.wait_ge(probs_ready, u + 1)
                if u >= 2:
                    dve.wait_ge(head_copied, u - 1)
                inv = row_inv[:, u % 2, :]
                if u < HEADS // 2:
                    nc.vector.reciprocal(inv[:, 0:TT], row_sum[:, 0:TT]).then_inc(weights_ready, 1)
                    return
                link(nc.vector.reciprocal(inv, row_sum[:, :]))
                link(nc.vector.tensor_scalar(neg_lam_inv[:, :], inv[:, TT:2 * TT], lam[:, 1:2], None, ALU.mult))
                for t in range(TT):
                    s = nc.vector.tensor_scalar(masked[:, t, :], probs[:, 1, t, :], neg_lam_inv[:, t:t + 1], None, ALU.mult)
                link(s)
                if u > HEADS // 2:
                    dve.wait_ge(w_turned, u)
                for t in range(TT):
                    s = nc.vector.scalar_tensor_tensor(weights[:, t, :], probs[:, 0, t, :], inv[:, t:t + 1],
                                                       masked[:, t, :], ALU.mult, ALU.add)
                s.then_inc(weights_ready, 1)

            def norm_heads(g):
                dve.wait_ge(head_copied, HEADS_C * (g + 1))
                inverse_root(head_rstd[:, :], head_ss[:, :], HD)
                for n in range(HEADS_C):
                    for t in range(TT):
                        o = rows[:, g % 2, t, n * HD:(n + 1) * HD]
                        i = HEADS_C * t + n
                        s = nc.vector.scalar_tensor_tensor(o, o, head_rstd[:, i:i + 1], g_ao if g < 2 else g_bo,
                                                           ALU.mult, ALU.mult)
                s.then_inc(rows_ready, 1)

            def attention_step(s):
                u, phase = divmod(s, 3)
                if phase == 1 and u < HEADS:
                    maxima(u)

            def attention_late(s):
                u, phase = divmod(s, 3)
                if phase == 1:
                    if u < HEADS:
                        finish_weights(u)
                    if u and u % HEADS_C == 0:
                        norm_heads(u // HEADS_C - 1)
                if phase == 2 and u and u % HEADS_C == 0:
                    g = u // HEADS_C - 1
                    turn_split_lo(ROWS[R_MIX] + g, mix_hi, mix_lo, 4 * g, 0)

            for c in range(3):
                dve.wait_ge(x_landed[c], 32)
                gain_x(ROWS[R_NORM1] + c, c, max(c - 1, 0))
                split_lo(IN1, 0, 8, c, c + 1, PARTS_D)
                if c == 2:
                    dve.wait_ge(x_landed[3], 32)
                    gain_x(ROWS[R_NORM1] + 3, 3, 2)
                turn_split_lo(ROWS[R_NORM1] + c, h_hi, h_lo, 4 * c, xg_at[c])
            split_lo(IN1, 0, 8, 3, 4, PARTS_D)
            ffn(IN1, OUT1, ROWS[R_FFN1], 0, False)
            for g in range(GROUPS):
                for j in range(SEG):
                    s = SEG * (g - 1) + j - 1
                    if s >= 0:
                        attention_step(s)
                    v = 2 * (SEG * g + j) + 4
                    split_lo(QKV, 0, 0, v, v + 1, PARTS_D)
                    if s >= 0:
                        attention_late(s)
                    split_lo(QKV, 0, 0, v + 1, v + 2, PARTS_D)
                    if g == 0 and j == 1:
                        turn_split_lo(ROWS[R_NORMX] + 3, h_hi, h_lo, 12, xg_at[3])
                        norm_factor(1)
                    if j in (5, 9):
                        scale_qk(2 * g + (j - 5) // 4)
                    if g == 0 and j == 10:
                        negative_lambda()
            for s in range(SEG * (GROUPS - 1) - 1, SEG * GROUPS + 3):
                attention_step(s)
                v = s - SEG * (GROUPS - 1) + 1 + 4
                if v < SEG + 4:
                    split_lo(PROJ, 0, 0, v, v + 1, PARTS_D)
                attention_late(s)
            for v in range(SEG + 4, 2 * len(PROJ_ORDER) + 4):
                split_lo(PROJ, 0, 0, v, v + 1, PARTS_D)
                if v - 4 in XG_TURN:
                    c = XG_TURN[v - 4]
                    turn_split_lo(ROWS[R_NORM2] + c, h_hi, h_lo, 4 * c, xg_at[c])
                if v in XG_UPDATE:
                    c = XG_UPDATE[v]
                    update_x(PROJ, c, v - 3, 1.0)
                    if c == 0:
                        dve.wait_ge(gain_landed, 32)
                    r = ROWS[R_NORM2] + c
                    gain_x(r, c, r if c == 0 else r - 1)
            ffn(IN2, OUT2, ROWS[R_FFN2], 2, True)

        @block.gpsimd
        def _(pool):
            chain = [0]

            def link(ins):
                chain[0] += 1
                ins.then_inc(pool_chain, 1)
                pool.wait_ge(pool_chain, chain[0])

            pool.wait_ge(const_landed, 16 * 11)
            for m in range(2 * GROUPS):
                g, kind = divmod(m, 2)
                width = HD if g < 2 else SUB
                heads, half = NC // width, width // 8
                gain = ((g_aq, g_ak), (g_bq, g_bk))[g // 2][kind]
                cos, sin = rope[g // 2]
                whole = qkv[:, g % 2, kind, :, :].rearrange("p t (h d) -> p (t h) d", d=width)
                pool.wait_ge(qk_scaled, m + 1)
                link(nc.gpsimd.tensor_tensor(whole, whole, gain.unsqueeze(1).to_broadcast([P, TT * heads, width]),
                                             ALU.mult))
                rows4 = qkv[:, g % 2, kind, :, :].rearrange("p t (h d) -> p t h d", d=width)
                x1, x2 = rows4[:, :, :, 0:half], rows4[:, :, :, half:2 * half]
                temps = [rot[:, n, :].rearrange("p (t h r) -> p t h r", t=TT, h=heads) for n in range(4)]
                for n, (v, f) in enumerate(((x1, cos), (x2, sin), (x2, cos), (x1, sin))):
                    s = nc.gpsimd.tensor_tensor(temps[n], v, f.unsqueeze(2).to_broadcast([P, TT, heads, half]), ALU.mult)
                link(s)
                nc.gpsimd.tensor_tensor(x1, temps[0], temps[1], ALU.subtract)
                nc.gpsimd.tensor_tensor(x2, temps[2], temps[3], ALU.add).then_inc(qk_normed, 1)


_INS = ["x", "ffn1_norm", "ffn1_w_in", "ffn1_w_out", "mix_norm", "w_in", "a_q_norm", "a_k_norm", "b_q_norm",
        "b_k_norm", "lambda_q1", "lambda_k1", "lambda_q2", "lambda_k2", "a_out_norm", "b_out_norm", "w_out",
        "ffn2_norm", "ffn2_w_in", "ffn2_w_out"]


def kernel(**inputs):
    import concourse.bacc as bacc
    from concourse.bass_utils import run_bass_kernel_spmd

    nc = bacc.Bacc("TRN2", target_bir_lowering=False, num_devices=1, dynamic_dma_scratch_size=1024)
    arrays = {f"in_{name}": np.ascontiguousarray(inputs[name]) for name in _INS}
    arrays["in_consts"] = shape_constants()
    args = [nc.dram_tensor(n, a.shape, mybir.dt.from_np(a.dtype), kind="ExternalInput").ap()
            for n, a in arrays.items()]
    out = nc.dram_tensor("out_y", (1, SEQ, D), F32, kind="ExternalOutput").ap()
    hybrid_layer_kernel(nc, *args, out)
    r = run_bass_kernel_spmd(nc, [arrays], core_ids=[0])
    return r.results[0]["out_y"]
```

```python
from contextlib import ExitStack

import numpy as np

import concourse.bass as bass
from concourse import mybir

ALU = mybir.AluOpType
ACT = mybir.ActivationFunctionType
F32 = mybir.dt.float32
F32R = mybir.dt.float32r
I32 = mybir.dt.int32
AX_X = mybir.AxisListType.X

P = 128
SEQ = 256
TT = SEQ // P
D = 2048
FF = 5632
HD = 128
SUB = 64
NC = 512
KT = 4
KD = D // P
KF = FF // P
EPS = 1e-6
ROPE_THETA = 500000.0
PATTERNS = ((128, 1), (512, 4), (2048, 16))
SCALE_A = HD ** -0.5
SCALE_B = SUB ** -0.5
LAMBDA_INIT = 0.8 - 0.6 * float(np.exp(-0.3 * 0))
MASKED = -1e30
ROOT_MAGIC = 0x5F3759DF

RAW = 4
RING = 4
UK = 2
PARTS_D = [KT] * (KD // KT)
PARTS_F = [KT] * 8 + [3] * 4
assert sum(PARTS_F) == KF and len(PARTS_F) % RAW == 0
UNITS_D, UNITS_F = 2 * len(PARTS_D), 2 * len(PARTS_F)

FFN_ITERS = FF // NC
HEADS_C = NC // HD
GROUP_AT = (2, 3, 0, 1)
GROUPS = len(GROUP_AT)
B_GROUPS = 2
HEADS = GROUPS * HEADS_C
B_HEADS = B_GROUPS * HEADS_C
SEG = 3 * len(PARTS_D)

N_IN, N_OUT, N_QKV, N_PROJ = FFN_ITERS * 8, 4 * len(PARTS_F), GROUPS * SEG, 4 * len(PARTS_D)
PROJ_ORDER = [(c, j) for j in range(3) for c in (0, 1)] + [(2, 0), (2, 1), (2, 2), (0, 3), (1, 3), (2, 3)] + [(3, j) for j in range(4)]
PROJ_BANK = (0, 1, 2, 1)
PIECE = np.cumsum([0, N_IN, N_OUT, N_QKV, N_PROJ, N_IN, N_OUT]).tolist()
READS = np.cumsum([[0, 0, 0], [FFN_ITERS, 0, 0], [2, 2, 0], [6, 6, 0], [1, 2, 1], [FFN_ITERS, 0, 0], [2, 2, 0]], axis=0).tolist()
IN1, OUT1, QKV, PROJ, IN2, OUT2 = range(6)
ROWS = np.cumsum([0, 4, FFN_ITERS, 4, 4, 4, FFN_ITERS]).tolist()
R_NORM1, R_FFN1, R_NORMX, R_MIX, R_NORM2, R_FFN2 = range(6)


TAIL = (0, 1, 1, 1, 1, 1, 2, 1, 1, 1, 1, 1, 1, 1, 2)
assert len(TAIL) == SEG + 3 and sum(TAIL) <= 2 * PROJ_ORDER.index((0, 3))
assert sum(TAIL[:SEG - 1]) <= 2 * PROJ_ORDER.index((2, 0))

XG_TURN = {21: 0, 24: 1, 27: 2}
XG_UPDATE = {23: 0, 25: 1, 27: 2, 35: 3}
XG_SQUARE = {24: 0, 26: 1, 29: 2}


def shape_constants():
    q, k = np.arange(SEQ)[:, None], np.arange(SEQ)[None, :]
    held = sum(((k - q) % d == 0) & (abs(k - q) <= w // 2) for w, d in PATTERNS)
    mask = np.where(held > 0, np.log(np.maximum(held, 1)) / SCALE_A, MASKED).astype(np.float32)
    parts = [np.eye(P, dtype=np.float32), mask.reshape(TT, P, SEQ).transpose(1, 0, 2).reshape(P, -1)]
    for width in (HD, SUB):
        rd = width // 4
        inv = (np.float32(ROPE_THETA) ** (-np.arange(0, rd, 2, dtype=np.float32) / np.float32(rd))).astype(np.float32)
        ang = np.arange(SEQ, dtype=np.float32)[:, None] * inv[None, :]
        for f in (np.cos, np.sin):
            parts.append(f(ang).astype(np.float32).reshape(TT, P, rd // 2).transpose(1, 0, 2).reshape(P, -1))
    return np.ascontiguousarray(np.concatenate(parts, axis=1))


N_CONST = P + TT * SEQ + 2 * TT * 16 + 2 * TT * 8


def hybrid_layer_kernel(nc, x, ffn1_norm, ffn1_w_in, ffn1_w_out, mix_norm, w_in, a_q_norm, a_k_norm, b_q_norm,
                        b_k_norm, lambda_q1, lambda_k1, lambda_q2, lambda_k2, a_out_norm, b_out_norm, w_out,
                        ffn2_norm, ffn2_w_in, ffn2_w_out, consts, out):
    x_dram = x[0].rearrange("(t p) d -> p t d", p=P)
    out_dram = out[0].rearrange("(t p) d -> p t d", p=P)

    def tiled(w):
        return w[0].rearrange("(c p) n -> p c n", p=P)

    with ExitStack() as ctx:
        def sb(name, shape, dt=F32, stack=ctx):
            return stack.enter_context(nc.sbuf_tensor(name, shape, dt))

        def sem(name):
            return ctx.enter_context(nc.semaphore(name))

        x_sb = sb("x_sb", [P, TT, D])
        rows = sb("rows", [P, 2, TT, NC])
        gain_row = sb("gain_row", [P, D])
        h_hi = sb("h_hi", [P, KD, SEQ], F32R)
        h_lo = sb("h_lo", [P, KD, SEQ], F32R)
        w_raw = sb("w_raw", [P, RAW, KT, NC])
        w_hi = sb("w_hi", [P, RING, UK, NC], F32R)
        w_lo = sb("w_lo", [P, RING, UK, NC], F32R)
        cst = sb("cst", [P, N_CONST])
        gains = sb("gains", [P, 4 * HD + 2 * SUB])
        dump = sb("dump", [P, NC], mybir.dt.bfloat16)
        sumsq = sb("sumsq", [P, TT, 4])
        rstd = sb("rstd", [P, TT])
        lam = sb("lam", [P, 4])
        root = sb("root", [P, 48])

        with ExitStack() as hidden:
            act_hi = sb("act_hi", [P, KF, SEQ], F32R, hidden)
            act_lo = sb("act_lo", [P, KF, SEQ], F32R, hidden)
        with ExitStack() as attention:
            mix_hi = sb("mix_hi", [P, KD, SEQ], F32R, attention)
            mix_lo = sb("mix_lo", [P, KD, SEQ], F32R, attention)
            qkv = sb("qkv", [P, 2, 3, TT, NC], F32, attention)
            squares = sb("squares", [P, TT, NC], F32, attention)
            rot = sb("rot", [P, 4, P], F32, attention)
            masked = sb("masked", [P, TT, SEQ], F32, attention)
            probs = sb("probs", [P, 2, TT, SEQ], F32, attention)
            weights = sb("weights", [P, TT, SEQ], F32, attention)
            qk_t = sb("qk_t", [P, 2, SEQ], F32, attention)
            w_t = sb("w_t", [P, TT, SEQ], F32, attention)
            head_sq = sb("head_sq", [P, TT, HD], F32, attention)
            head_ss = sb("head_ss", [P, TT * HEADS_C], F32, attention)
            head_rstd = sb("head_rstd", [P, TT * HEADS_C], F32, attention)
            lam_in = sb("lam_in", [P, 4, SUB], F32, attention)
            lam_prod = sb("lam_prod", [P, 2, SUB], F32, attention)
            qk_ss = sb("qk_ss", [P, TT * 8], F32, attention)
            qk_rstd = sb("qk_rstd", [P, TT * 8], F32, attention)
            row_max = sb("row_max", [P, 4], F32, attention)
            neg_max = sb("neg_max", [P, 4], F32, attention)
            row_sum = sb("row_sum", [P, 4], F32, attention)
            row_inv = sb("row_inv", [P, 2, 4], F32, attention)
            neg_lam_inv = sb("neg_lam_inv", [P, 2], F32, attention)

        acc = [ctx.enter_context(nc.psum_tensor(f"acc{i}", [P, TT, NC], F32)) for i in range(2)]
        turn = [ctx.enter_context(nc.psum_tensor(f"turn{i}", [P, TT * NC], F32)) for i in range(2)]
        turn4 = [t[:, :].rearrange("p (k s) -> p k s", s=SEQ) for t in turn]
        qk_turn = turn[0][:, 0:NC].rearrange("p (a s) -> p a s", s=SEQ)
        head_acc = turn[0][:, 0:TT * HD].rearrange("p (t d) -> p t d", d=HD)
        w_turn = turn[0][:, NC:2 * NC].rearrange("p (a s) -> p a s", s=SEQ)
        score = turn[1][:, :].rearrange("p (c t s) -> p c t s", t=TT, s=SEQ)

        banks = acc + [turn[1][:, :].rearrange("p (t n) -> p t n", n=NC)]

        ident = cst[:, 0:P]
        at = P
        mask = cst[:, at:at + TT * SEQ].rearrange("p (t s) -> p t s", t=TT)
        at += TT * SEQ
        rope = []
        for half in (16, 8):
            table = cst[:, at:at + 2 * TT * half].rearrange("p (f t r) -> p f t r", f=2, t=TT)
            rope.append((table[:, 0], table[:, 1]))
            at += 2 * TT * half
        g_aq, g_ak, g_ao, g_bo = (gains[:, HD * i:HD * (i + 1)] for i in range(4))
        g_bq, g_bk = (gains[:, 4 * HD + SUB * i:4 * HD + SUB * (i + 1)] for i in range(2))

        x_landed = [sem(f"x_landed{c}") for c in range(4)]
        ident_landed = sem("ident_landed")
        const_landed = sem("const_landed")
        gain_landed = sem("gain_landed")
        raw_landed = [sem(f"raw_landed{i}") for i in range(RAW)]
        hi_ready = sem("hi_ready")
        lo_ready = sem("lo_ready")
        units_used = sem("units_used")
        bank_free = [sem(f"bank_free{i}") for i in range(3)]
        rows_ready = sem("rows_ready")
        rows_turned = sem("rows_turned")
        turn_hi = sem("turn_hi")
        turn_split = sem("turn_split")
        x_squared = sem("x_squared")
        dve_chain = sem("dve_chain")
        pool_chain = sem("pool_chain")
        rstd_ready = sem("rstd_ready")
        lam_sums = sem("lam_sums")
        lam_exps = sem("lam_exps")
        qk_squared = sem("qk_squared")
        qk_summed = sem("qk_summed")
        qk_scaled = sem("qk_scaled")
        qk_normed = sem("qk_normed")
        qk_turned = sem("qk_turned")
        qk_t_ready = sem("qk_t_ready")
        scored = sem("scored")
        max_ready = sem("max_ready")
        probs_ready = sem("probs_ready")
        weights_ready = sem("weights_ready")
        w_turned = sem("w_turned")
        w_t_ready = sem("w_t_ready")
        head_done = sem("head_done")
        head_moved = sem("head_moved")
        head_copied = sem("head_copied")
        stored = sem("stored")

        def place(stage, q):
            if stage == PROJ:
                return PROJ_BANK[q], PROJ_BANK[:q].count(PROJ_BANK[q])
            return q % 2, q // 2

        def wait_read(eng, stage, q):
            b, before = place(stage, q)
            eng.wait_ge(bank_free[b], READS[stage][b] + before + 1)

        def turned_at(s):
            u, phase = divmod(s, 3)
            return phase == 2 and (u == HEADS or u % HEADS_C == 1 and u > 1)

        def unit_k(parts, v):
            k0, count = sum(parts[:v // 2]), parts[v // 2]
            return (k0 + UK, count - UK) if v % 2 else (k0, UK)

        def tail():
            return [(SEG * (GROUPS - 1) + i, sum(TAIL[:i]), count) for i, count in enumerate(TAIL)]

        xg_at = [1, 0, 1, 0]

        block = ctx.enter_context(nc.Block())

        @block.sync
        def _(sp):
            def load(src, col, k0, count, p, j):
                if not isinstance(p, int) or p >= RAW:
                    sp.wait_ge(lo_ready, (p - RAW + 1) * 2)
                sp.dma_start(w_raw[:, j % RAW, 0:count, :],
                             src[:, k0:k0 + count, bass.ds(col, NC)]).then_inc(raw_landed[j % RAW], 16)

            def load_chunk(src, col, parts, p0):
                for j, count in enumerate(parts):
                    load(src, col, sum(parts[:j]), count, p0 + j, j)

            def ffn(w1, w2, s_in, s_out, started, gain, norms):
                gate_up = tiled(w1)
                with sp.Fori(started, FFN_ITERS) as i:
                    load_chunk(gate_up, i * NC, PARTS_D, i * 8 + PIECE[s_in])
                    load_chunk(gate_up, i * NC + FF, PARTS_D, i * 8 + PIECE[s_in] + 4)
                if gain is not None:
                    sp.wait_ge(rows_ready, norms)
                    sp.dma_start(gain_row[:, :], gain.to_broadcast([P, D])).then_inc(gain_landed, 16)
                down = tiled(w2)
                with sp.Fori(0, 4) as n:
                    load_chunk(down, n * NC, PARTS_F, n * len(PARTS_F) + PIECE[s_out])

            gate_up1 = tiled(ffn1_w_in)
            for c in range(4):
                cols = slice(c * NC, (c + 1) * NC)
                sp.dma_start(x_sb[:, :, cols], x_dram[:, :, cols]).then_inc(x_landed[c], 16)
                sp.dma_start(gain_row[:, cols], ffn1_norm[:, cols].to_broadcast([P, NC])).then_inc(x_landed[c], 16)
                if c:
                    load(gate_up1, 0, KT * (c - 1), KT, c - 1, c - 1)
            load(gate_up1, 0, KT * 3, KT, 3, 3)
            sp.dma_start(cst[:, P:N_CONST], consts[:, P:N_CONST]).then_inc(const_landed, 16)
            for gain, dst in ((a_q_norm, g_aq), (a_k_norm, g_ak), (a_out_norm, g_ao), (b_out_norm, g_bo),
                              (b_q_norm, g_bq), (b_k_norm, g_bk)):
                sp.dma_start(dst, gain.to_broadcast([P, gain.shape[1]])).then_inc(const_landed, 16)
            for n, vec in enumerate((lambda_q1, lambda_k1, lambda_q2, lambda_k2)):
                sp.dma_start(lam_in[:, n, :], vec.to_broadcast([P, SUB])).then_inc(const_landed, 16)
            load_chunk(gate_up1, FF, PARTS_D, 4)
            ffn(ffn1_w_in, ffn1_w_out, IN1, OUT1, 1, mix_norm, 4)
            qkv_w = tiled(w_in)
            for g in range(GROUPS):
                base = (GROUP_AT[g] // 2) * 3 * (D // 2) + (GROUP_AT[g] % 2) * NC
                for kind in range(3):
                    load_chunk(qkv_w, base + kind * (D // 2), PARTS_D, PIECE[QKV] + SEG * g + 4 * kind)
            sp.wait_ge(rows_ready, ROWS[R_MIX])
            sp.dma_start(gain_row[:, :], ffn2_norm.to_broadcast([P, D])).then_inc(gain_landed, 16)
            proj_w = tiled(w_out)
            for n, (c, j) in enumerate(PROJ_ORDER):
                load(proj_w, c * NC, GROUP_AT[j] * KT, KT, PIECE[PROJ] + n, n)
            ffn(ffn2_w_in, ffn2_w_out, IN2, OUT2, 0, None, None)
            for c in range(4):
                wait_read(sp, OUT2, c)
                sp.dma_start(out_dram[:, :, c * NC:(c + 1) * NC],
                             x_sb[:, :, c * NC:(c + 1) * NC]).then_inc(stored, 16)
            sp.wait_ge(stored, 64)

        @block.tensor
        def _(pe):
            def unit(u, slot, k0, count, lhs, bank, first, last):
                pe.wait_ge(lo_ready, u + 1)
                for kk in range(count):
                    for t in range(TT):
                        hi, lo = (a[:, k0 + kk, t * P:(t + 1) * P] for a in lhs)
                        o = banks[bank][:, t, :]
                        nc.tensor.matmul(o, hi, w_hi[:, slot, kk, :], start=first and kk == 0, stop=False)
                        nc.tensor.matmul(o, hi, w_lo[:, slot, kk, :], start=False, stop=False)
                        mm = nc.tensor.matmul(o, lo, w_hi[:, slot, kk, :], start=False,
                                              stop=last and kk == count - 1)
                mm.then_inc(units_used, 1)

            def chunk(parts, u0, vs, lhs, bank, split=None):
                for v in vs:
                    if split is not None and v % 2 == 0:
                        pe.wait_ge(turn_split, split + v // 2 + 1)
                    k0, count = unit_k(parts, v)
                    unit(u0 + v, v % RING, k0, count, lhs, bank, v == 0, v == 2 * len(parts) - 1)

            def bank_wait(stage, b, uses):
                if not isinstance(uses, int) or READS[stage][b] + uses:
                    pe.wait_ge(bank_free[b], uses + READS[stage][b])

            def turn_rows(r, buf, split, pair=None):
                pair = buf if pair is None else pair
                pe.wait_ge(rows_ready, r + 1)
                if split is not None:
                    pe.wait_ge(turn_split, split)
                for k in range(4):
                    for t in range(TT):
                        mm = nc.tensor.transpose(turn4[pair][:, k, t * P:(t + 1) * P],
                                                 rows[:, buf, t, k * P:(k + 1) * P], ident)
                mm.then_inc(rows_turned, 1)

            h, act = (h_hi, h_lo), (act_hi, act_lo)

            def hidden(s_in, i, r0, first):
                u0 = i * 16 + 2 * PIECE[s_in]
                bank_wait(s_in, 0, i)
                if first and s_in == IN1:
                    chunk(PARTS_D, u0, range(1), h, 0, r0 - 4)
                    turn_rows(r0 - 2, xg_at[2], r0 - 3)
                    chunk(PARTS_D, u0, range(1, 4), h, 0, r0 - 4)
                else:
                    chunk(PARTS_D, u0, range(4), h, 0, r0 - 4 if first else None)
                turn_rows(i + (r0 - 1), 0, i + (r0 - 1))
                chunk(PARTS_D, u0, range(4, 8), h, 0, r0 - 4 if first else None)
                if first:
                    bank_wait(s_in, 1, 0)
                else:
                    pe.wait_ge(rows_ready, i + r0)
                chunk(PARTS_D, u0 + 8, range(8), h, 1)

            def down(s_out, i, r0, turns):
                for b in range(2):
                    u0 = i * (2 * UNITS_F) + 2 * PIECE[s_out] + b * UNITS_F
                    bank_wait(s_out, b, i)
                    chunk(PARTS_F, u0, range(4), act, b)
                    if b < turns:
                        r = i * 2 + (r0 + FFN_ITERS - 1 + b)
                        turn_rows(r, b, r - b)
                    chunk(PARTS_F, u0, range(4, 20), act, b)
                    pe.wait_ge(turn_split, r0 + FFN_ITERS)
                    chunk(PARTS_F, u0, range(20, UNITS_F), act, b)

            def ffn(s_in, s_out, r0, final):
                hidden(s_in, 0, r0, True)
                with pe.Fori(1, FFN_ITERS) as i:
                    hidden(s_in, i, r0, False)
                if final:
                    down(s_out, 0, r0, 1)
                    down(s_out, 1, r0, 0)
                else:
                    with pe.Fori(0, 2) as i:
                        down(s_out, i, r0, 2)

            def turn_qk(u):
                g, n = divmod(u, HEADS_C)
                pe.wait_ge(qk_normed, 2 * g + 2)
                if u >= 2:
                    pe.wait_ge(head_copied, u - 1)
                for a in range(2):
                    for t in range(TT):
                        mm = nc.tensor.transpose(qk_turn[:, a, t * P:(t + 1) * P],
                                                 qkv[:, g % 2, a, t, n * HD:(n + 1) * HD], ident)
                mm.then_inc(qk_turned, 1)

            def scores(u):
                pe.wait_ge(qk_t_ready, u + 1)
                if u:
                    pe.wait_ge(probs_ready, u)
                subs = 2 if u < B_HEADS else 1
                width = HD // subs
                for c in range(subs):
                    part = slice(c * width, (c + 1) * width)
                    for t in range(TT):
                        mm = nc.tensor.matmul(score[:, c, t, :], qk_t[part, 0, t * P:(t + 1) * P],
                                              qk_t[part, 1, :], start=True, stop=True)
                mm.then_inc(scored, 1)

            def turn_weights(u):
                pe.wait_ge(weights_ready, u + 1)
                src = weights if u < B_HEADS else probs[:, 0]
                for kt in range(TT):
                    for t in range(TT):
                        mm = nc.tensor.transpose(w_turn[:, kt, t * P:(t + 1) * P],
                                                 src[:, t, kt * P:(kt + 1) * P], ident)
                mm.then_inc(w_turned, 1)

            def values(u):
                g, n = divmod(u, HEADS_C)
                pe.wait_ge(w_t_ready, u + 1)
                wait_read(pe, QKV, 3 * g + 2)
                if u + 1 < HEADS:
                    pe.wait_ge(qk_t_ready, u + 2)
                for t in range(TT):
                    for kt in range(TT):
                        mm = nc.tensor.matmul(head_acc[:, t, :], w_t[:, kt, t * P:(t + 1) * P],
                                              qkv[:, g % 2, 2, kt, n * HD:(n + 1) * HD],
                                              start=kt == 0, stop=kt == TT - 1)
                mm.then_inc(head_done, 1)

            def attention_step(s):
                u, phase = divmod(s, 3)
                if phase == 0:
                    if u % HEADS_C == 2 and u > 2:
                        pe.wait_ge(turn_split, ROWS[R_MIX] + u // HEADS_C)
                    if 1 <= u <= HEADS:
                        turn_weights(u - 1)
                    if u < HEADS:
                        turn_qk(u)
                if phase == 1:
                    if 1 <= u <= HEADS:
                        values(u - 1)
                    if u < HEADS:
                        scores(u)
                if turned_at(s):
                    g = u // HEADS_C - 1
                    pe.wait_ge(head_copied, u)
                    pe.wait_ge(rows_ready, ROWS[R_MIX] + g + 1)
                    for k in range(4):
                        for t in range(TT):
                            mm = nc.tensor.transpose(turn4[0][:, k, t * P:(t + 1) * P],
                                                     rows[:, g % 2, t, k * P:(k + 1) * P], ident)
                    mm.then_inc(rows_turned, 1)

            def project(n):
                c, j = PROJ_ORDER[n // 2]
                v = 2 * j + n % 2
                bank, before = place(PROJ, c)
                if v == 0 and bank < 2:
                    bank_wait(PROJ, bank, before)
                elif v == 0:
                    pe.wait_ge(max_ready, HEADS)
                if v % 2 == 0:
                    pe.wait_ge(turn_split, ROWS[R_MIX] + j + 1)
                k0, count = unit_k(PARTS_D, v)
                unit(2 * PIECE[PROJ] + n, n % RING, k0, count, (mix_hi, mix_lo), bank, v == 0, v == UNITS_D - 1)

            pe.wait_ge(ident_landed, 16)
            for c in range(2):
                turn_rows(ROWS[R_NORM1] + c, xg_at[c], None)
            ffn(IN1, OUT1, ROWS[R_FFN1], False)
            for g in range(GROUPS):
                for j in range(SEG):
                    q = 3 * g + j // 4
                    if j % 4 == 0:
                        bank_wait(QKV, q % 2, q // 2)
                    chunk(PARTS_D, 2 * PIECE[QKV] + 8 * q, range(2 * (j % 4), 2 * (j % 4) + 2), h, q % 2,
                          ROWS[R_NORMX] if q == 0 else None)
                    if g == 0 and j == 1:
                        turn_rows(ROWS[R_NORMX] + 3, xg_at[3], ROWS[R_NORMX] + 2)
                    if g:
                        attention_step(SEG * (g - 1) + j)
            for s, n, count in tail():
                for m in range(count):
                    project(n + m)
                attention_step(s)
            for n in range(sum(TAIL), 2 * len(PROJ_ORDER)):
                project(n)
                if n in XG_TURN:
                    c = XG_TURN[n]
                    turn_rows(ROWS[R_NORM2] + c, xg_at[c], ROWS[R_NORM2] + c, 0)
            ffn(IN2, OUT2, ROWS[R_FFN2], True)

        @block.scalar
        def _(act):
            def split_hi(stage, i, per, first, last, parts):
                for v in range(first, last):
                    u = i * (2 * per) + 2 * PIECE[stage] + v
                    count = unit_k(parts, v % (2 * len(parts)))[1]
                    act.wait_ge(raw_landed[v // 2 % RAW],
                                i * (per // RAW * 16) + (PIECE[stage] // RAW + v // 2 // RAW + 1) * 16)
                    if not isinstance(u, int) or u >= RING:
                        act.wait_ge(units_used, u - RING + 1)
                    k0 = v % 2 * UK
                    nc.scalar.activation(w_hi[:, v % RING, 0:count, :], w_raw[:, v // 2 % RAW, k0:k0 + count, :],
                                         ACT.Copy).then_inc(hi_ready, 1)

            def turn_split_hi(r, dst, k, pair):
                act.wait_ge(rows_turned, r + 1)
                nc.scalar.activation(dst[:, bass.ds(k, 4), :], turn4[pair], ACT.Copy).then_inc(turn_hi, 1)

            def square_x(n, c):
                for t in range(TT):
                    before = 2 * (4 * n + c) + t
                    if before:
                        act.wait_ge(x_squared, before)
                    nc.scalar.activation(dump[:, :], x_sb[:, t, c * NC:(c + 1) * NC],
                                         ACT.Square, accum_out=sumsq[:, t, c:c + 1]).then_inc(x_squared, 1)

            def silu(s_in, i):
                act.wait_ge(units_used, i * 16 + 2 * PIECE[s_in] + 8)
                for t in range(TT):
                    s = nc.scalar.activation(rows[:, 0, t, :], acc[0][:, t, :], ACT.Silu, scale=rstd[:, t:t + 1])
                s.then_inc(bank_free[0], 1)

            def ffn(s_in, s_out, r0, n, updated, final):
                split_hi(s_in, 0, 8, 4, 6, PARTS_D)
                updated()
                square_x(n, 3)
                split_hi(s_in, 0, 8, 6, 8, PARTS_D)
                turn_split_hi(r0 - 1, h_hi, 12, 0)
                split_hi(s_in, 0, 8, 8, 12, PARTS_D)
                act.wait_ge(rstd_ready, n + 1)
                silu(s_in, 0)
                split_hi(s_in, 0, 8, 12, 20, PARTS_D)
                with act.Fori(1, FFN_ITERS) as i:
                    split_hi(s_in, i, 8, 4, 8, PARTS_D)
                    turn_split_hi(i + (r0 - 1), act_hi, i * 4 - 4, 0)
                    split_hi(s_in, i, 8, 8, 12, PARTS_D)
                    silu(s_in, i)
                    split_hi(s_in, i, 8, 12, 20, PARTS_D)
                for c in range(4):
                    first = c * UNITS_F
                    split_hi(s_out, 0, 0, first + 4, first + 6, PARTS_F)
                    if c and not final:
                        wait_read(act, s_out, c - 1)
                        square_x(n + 1, c - 1)
                    split_hi(s_out, 0, 0, first + 6, first + 8, PARTS_F)
                    r = r0 + FFN_ITERS - 1 + c
                    if c == 0:
                        turn_split_hi(r, act_hi, KF - 4, 0)
                    elif not final:
                        turn_split_hi(r, h_hi, 4 * (c - 1), xg_at[c - 1])
                    last = first + UNITS_F if final and c == 3 else first + UNITS_F + 4
                    split_hi(s_out, 0, 0, first + 8, last, PARTS_F)

            def copy_chunk(q):
                g, kind = divmod(q, 3)
                act.wait_ge(units_used, 2 * PIECE[QKV] + UNITS_D * (q + 1))
                if g >= 2:
                    if kind < 2:
                        act.wait_ge(qk_turned, HEADS_C * (g - 1))
                    else:
                        act.wait_ge(head_done, HEADS_C * (g - 1))
                for t in range(TT):
                    s = nc.scalar.activation(qkv[:, g % 2, kind, t, :], acc[q % 2][:, t, :], ACT.Copy,
                                             scale=rstd[:, t:t + 1])
                s.then_inc(bank_free[q % 2], 1)
                if kind < 2:
                    m = 2 * g + kind
                    if m:
                        act.wait_ge(qk_summed, m)
                    wait_read(act, QKV, q)
                    nc.scalar.activation(squares[:, :, :], qkv[:, g % 2, kind, :, :], ACT.Square).then_inc(qk_squared, 1)

            def copy_qk_t(u):
                act.wait_ge(qk_turned, u + 1)
                if u:
                    act.wait_ge(scored, u)
                nc.scalar.activation(qk_t[:, :, :], qk_turn, ACT.Copy).then_inc(qk_t_ready, 1)

            def exps(u):
                act.wait_ge(max_ready, u + 1)
                if u:
                    act.wait_ge(w_turned, u)
                    act.wait_ge(weights_ready, u)
                subs = 2 if u < B_HEADS else 1
                for c in range(subs):
                    for t in range(TT):
                        i = TT * c + t
                        src = masked[:, t, :] if subs == 1 else score[:, c, t, :]
                        s = nc.scalar.activation(probs[:, c, t, :], src, ACT.Exp, bias=neg_max[:, i:i + 1],
                                                 scale=SCALE_A if subs == 1 else SCALE_B,
                                                 accum_out=row_sum[:, i:i + 1])
                s.then_inc(probs_ready, 1)

            def copy_w_t(u):
                act.wait_ge(w_turned, u + 1)
                if u:
                    act.wait_ge(head_done, u)
                nc.scalar.activation(w_t[:, :, :], w_turn, ACT.Copy).then_inc(w_t_ready, 1)

            def copy_head(u):
                g, n = divmod(u, HEADS_C)
                act.wait_ge(head_done, u + 1)
                if n == 0:
                    act.wait_ge(rows_turned, ROWS[R_MIX] + max(g - 1, 0))
                    act.wait_ge(rows_ready, ROWS[R_MIX] + g)
                if u:
                    act.wait_ge(head_copied, u)
                for t in range(TT):
                    scale = 1.0 if u < B_HEADS else row_inv[:, u % 2, t:t + 1]
                    s = nc.scalar.activation(rows[:, g % 2, t, n * HD:(n + 1) * HD], head_acc[:, t, :], ACT.Copy,
                                             scale=scale)
                s.then_inc(head_moved, 1)
                act.wait_ge(head_moved, u + 1)
                for t in range(TT):
                    i = TT * n + t
                    s = nc.scalar.activation(head_sq[:, t, :], rows[:, g % 2, t, n * HD:(n + 1) * HD], ACT.Square,
                                             accum_out=head_ss[:, i:i + 1])
                s.then_inc(head_copied, 1)

            def attention_step(s):
                u, phase = divmod(s, 3)
                if phase == 0:
                    if u < HEADS:
                        copy_qk_t(u)
                    if 1 <= u <= HEADS:
                        copy_w_t(u - 1)
                if phase == 1:
                    if 1 <= u <= HEADS:
                        copy_head(u - 1)
                    if u < HEADS:
                        exps(u)
                if turned_at(s):
                    g = u // HEADS_C - 1
                    turn_split_hi(ROWS[R_MIX] + g, mix_hi, 4 * g, 0)

            act.dma_start(cst[:, 0:P], consts[:, 0:P]).then_inc(ident_landed, 16)
            for c in range(2):
                turn_split_hi(ROWS[R_NORM1] + c, h_hi, 4 * c, xg_at[c])
                split_hi(IN1, 0, 8, c, c + 1, PARTS_D)
            for c in range(2):
                act.wait_ge(x_landed[c], 32)
                square_x(0, c)
            split_hi(IN1, 0, 8, 2, 3, PARTS_D)
            turn_split_hi(ROWS[R_NORM1] + 2, h_hi, 8, xg_at[2])
            split_hi(IN1, 0, 8, 3, 4, PARTS_D)
            act.wait_ge(x_landed[2], 32)
            square_x(0, 2)
            ffn(IN1, OUT1, ROWS[R_FFN1], 0, lambda: act.wait_ge(x_landed[3], 32), False)
            for g in range(GROUPS):
                for j in range(SEG):
                    if j % 4 == 0 and 3 * g + j // 4 > 0:
                        copy_chunk(3 * g + j // 4 - 1)
                    s = SEG * (g - 1) + j - 1
                    if s >= 0:
                        attention_step(s)
                    v = 2 * (SEG * g + j) + 4
                    split_hi(QKV, 0, 0, v, v + 2, PARTS_D)
                    if g == 0 and j == 0:
                        wait_read(act, OUT1, 3)
                        square_x(1, 3)
                    if g == 0 and j == 1:
                        turn_split_hi(ROWS[R_NORMX] + 3, h_hi, 12, xg_at[3])
                        act.wait_ge(rstd_ready, 2)
                    if g == 0 and j == 2:
                        act.wait_ge(lam_sums, 1)
                        nc.scalar.activation(lam[:, 2:4], lam[:, 0:2], ACT.Exp).then_inc(lam_exps, 1)
            copy_chunk(3 * GROUPS - 1)
            for s, n, count in tail():
                attention_step(s - 1)
                split_hi(PROJ, 0, 0, n + 4, n + count + 4, PARTS_D)
            attention_step(SEG * GROUPS + 2)
            for v in range(sum(TAIL) + 4, 2 * len(PROJ_ORDER) + 4):
                split_hi(PROJ, 0, 0, v, v + 1, PARTS_D)
                if v in XG_SQUARE:
                    wait_read(act, PROJ, XG_SQUARE[v])
                    square_x(2, XG_SQUARE[v])
                if v - 4 in XG_TURN:
                    c = XG_TURN[v - 4]
                    turn_split_hi(ROWS[R_NORM2] + c, h_hi, 4 * c, 0)
            ffn(IN2, OUT2, ROWS[R_FFN2], 2, lambda: wait_read(act, PROJ, 3), True)

        @block.vector
        def _(dve):
            chain = [0]

            def link(ins):
                chain[0] += 1
                ins.then_inc(dve_chain, 1)
                dve.wait_ge(dve_chain, chain[0])

            def split_lo(stage, i, per, first, last, parts):
                for v in range(first, last):
                    u = i * (2 * per) + 2 * PIECE[stage] + v
                    count = unit_k(parts, v % (2 * len(parts)))[1]
                    dve.wait_ge(hi_ready, u + 1)
                    k0 = v % 2 * UK
                    nc.vector.tensor_tensor(w_lo[:, v % RING, 0:count, :], w_raw[:, v // 2 % RAW, k0:k0 + count, :],
                                            w_hi[:, v % RING, 0:count, :].bitcast(F32),
                                            ALU.subtract).then_inc(lo_ready, 1)

            def turn_split_lo(r, dst_hi, dst_lo, k, pair):
                dve.wait_ge(turn_hi, r + 1)
                nc.vector.tensor_tensor(dst_lo[:, bass.ds(k, 4), :], turn4[pair],
                                        dst_hi[:, bass.ds(k, 4), :].bitcast(F32),
                                        ALU.subtract).then_inc(turn_split, 1)

            def inverse_root(y, src, width, done=None, count=0):
                n = y.shape[1]
                mean, square, bits = root[:, 0:n], root[:, 16:16 + n], root[:, 32:32 + n].bitcast(I32)
                link(nc.vector.tensor_scalar(mean, src, 1.0 / width, EPS, ALU.mult, ALU.add))
                link(nc.vector.tensor_scalar(bits, mean.bitcast(I32), 1, None, ALU.arith_shift_right))
                link(nc.vector.tensor_scalar(y.bitcast(I32), bits, -1, ROOT_MAGIC, ALU.mult, ALU.add))
                for step in range(3):
                    link(nc.vector.tensor_tensor(square, y, y, ALU.mult))
                    link(nc.vector.scalar_tensor_tensor(square, square, -0.5, mean, ALU.mult, ALU.mult))
                    last = nc.vector.scalar_tensor_tensor(y, square, 1.5, y, ALU.add, ALU.mult)
                    if step < 2 or done is None:
                        link(last)
                    else:
                        last.then_inc(done, 1)
                        dve.wait_ge(done, count)

            def norm_factor(n):
                dve.wait_ge(x_squared, 8 * (n + 1))
                link(nc.vector.tensor_reduce(rstd[:, :], sumsq[:, :, :], AX_X, ALU.add))
                inverse_root(rstd[:, :], rstd[:, :], D, rstd_ready, n + 1)

            def gain_x(r, c, turned):
                if turned:
                    dve.wait_ge(rows_turned, turned)
                cols = slice(c * NC, (c + 1) * NC)
                nc.vector.tensor_tensor(rows[:, xg_at[c], :, :], x_sb[:, :, cols],
                                        gain_row[:, cols].unsqueeze(1).to_broadcast([P, TT, NC]),
                                        ALU.mult).then_inc(rows_ready, 1)

            def product(s_in, i):
                dve.wait_ge(bank_free[0], i + READS[s_in][0] + 1)
                dve.wait_ge(units_used, i * 16 + 2 * PIECE[s_in] + 16)
                for t in range(TT):
                    s = nc.vector.scalar_tensor_tensor(rows[:, 0, t, :], acc[1][:, t, :], rstd[:, t:t + 1],
                                                       rows[:, 0, t, :], ALU.mult, ALU.mult)
                s.then_inc(rows_ready, 1)

            def update_x(stage, c, units, weight):
                dve.wait_ge(units_used, 2 * PIECE[stage] + units)
                bank = place(stage, c)[0]
                for t in range(TT):
                    o = x_sb[:, t, c * NC:(c + 1) * NC]
                    s = nc.vector.scalar_tensor_tensor(o, banks[bank][:, t, :], weight, o, ALU.mult, ALU.add)
                s.then_inc(bank_free[bank], 1)
                wait_read(dve, stage, c)

            def ffn(s_in, s_out, r0, n, final):
                split_lo(s_in, 0, 8, 4, 8, PARTS_D)
                turn_split_lo(r0 - 1, h_hi, h_lo, 12, 0)
                norm_factor(n)
                split_lo(s_in, 0, 8, 8, 20, PARTS_D)
                if n == 0:
                    lambda_sums()
                product(s_in, 0)
                with dve.Fori(1, FFN_ITERS) as i:
                    split_lo(s_in, i, 8, 4, 8, PARTS_D)
                    turn_split_lo(i + (r0 - 1), act_hi, act_lo, i * 4 - 4, 0)
                    split_lo(s_in, i, 8, 8, 20, PARTS_D)
                    product(s_in, i)
                for c in range(4):
                    first = c * UNITS_F
                    split_lo(s_out, 0, 0, first + 4, first + 8, PARTS_F)
                    r = r0 + FFN_ITERS - 1 + c
                    if c == 0:
                        turn_split_lo(r, act_hi, act_lo, KF - 4, 0)
                    elif not final:
                        turn_split_lo(r, h_hi, h_lo, 4 * (c - 1), xg_at[c - 1])
                    last = first + UNITS_F if final and c == 3 else first + UNITS_F + 4
                    split_lo(s_out, 0, 0, first + 8, last, PARTS_F)
                    update_x(s_out, c, UNITS_F * (c + 1), 0.5)
                    if not final:
                        if c == 0:
                            dve.wait_ge(gain_landed, 16)
                        gain_x(r + 1, c, r)

            def lambda_sums():
                dve.wait_ge(const_landed, 16 * 11)
                pairs = lam_in[:, :, :].rearrange("p (n two) d -> p n two d", two=2)
                link(nc.vector.tensor_tensor(lam_prod[:, :, :], pairs[:, :, 0, :], pairs[:, :, 1, :], ALU.mult))
                nc.vector.tensor_reduce(lam[:, 0:2], lam_prod[:, :, :], AX_X, ALU.add).then_inc(lam_sums, 1)
                link(nc.vector.tensor_scalar(g_bo, g_bo, 1.0 - LAMBDA_INIT, None, ALU.mult))

            def negative_lambda():
                dve.wait_ge(lam_exps, 1)
                link(nc.vector.tensor_tensor(lam[:, 0:1], lam[:, 3:4], lam[:, 2:3], ALU.subtract))
                link(nc.vector.tensor_scalar(lam[:, 1:2], lam[:, 0:1], -LAMBDA_INIT, None, ALU.add))

            def scale_qk(m):
                g, kind = divmod(m, 2)
                width = SUB if g < B_GROUPS else HD
                heads = NC // width
                ss, inv = qk_ss[:, 0:TT * heads], qk_rstd[:, 0:TT * heads]
                dve.wait_ge(qk_squared, m + 1)
                nc.vector.tensor_reduce(ss.rearrange("p (t h) -> p t h", t=TT),
                                        squares[:, :, :].rearrange("p t (h d) -> p t h d", d=width),
                                        AX_X, ALU.add).then_inc(qk_summed, 1)
                dve.wait_ge(qk_summed, m + 1)
                inverse_root(inv, ss, width)
                for t in range(TT):
                    o = qkv[:, g % 2, kind, t, :].rearrange("p (h d) -> p h d", d=width)
                    s = nc.vector.tensor_tensor(o, o, inv[:, t * heads:(t + 1) * heads].unsqueeze(2)
                                                .to_broadcast([P, heads, width]), ALU.mult)
                s.then_inc(qk_scaled, 1)

            def maxima(u):
                dve.wait_ge(scored, u + 1)
                if u:
                    dve.wait_ge(probs_ready, u)
                if u >= B_HEADS:
                    link(nc.vector.tensor_tensor(masked[:, :, :], score[:, 0], mask, ALU.add))
                    link(nc.vector.tensor_reduce(row_max[:, 0:TT], masked[:, :, :], AX_X, ALU.max))
                    nc.vector.tensor_scalar(neg_max[:, 0:TT], row_max[:, 0:TT], -SCALE_A, None,
                                            ALU.mult).then_inc(max_ready, 1)
                else:
                    link(nc.vector.tensor_reduce(row_max[:, :], score.rearrange("p c t s -> p (c t) s"), AX_X, ALU.max))
                    nc.vector.tensor_scalar(neg_max[:, :], row_max[:, :], -SCALE_B, None,
                                            ALU.mult).then_inc(max_ready, 1)

            def finish_weights(u):
                dve.wait_ge(probs_ready, u + 1)
                if u >= 2:
                    dve.wait_ge(head_copied, u - 1)
                inv = row_inv[:, u % 2, :]
                if u >= B_HEADS:
                    nc.vector.reciprocal(inv[:, 0:TT], row_sum[:, 0:TT]).then_inc(weights_ready, 1)
                    return
                link(nc.vector.reciprocal(inv, row_sum[:, :]))
                link(nc.vector.tensor_scalar(neg_lam_inv[:, :], inv[:, TT:2 * TT], lam[:, 1:2], None, ALU.mult))
                for t in range(TT):
                    s = nc.vector.tensor_scalar(masked[:, t, :], probs[:, 1, t, :], neg_lam_inv[:, t:t + 1], None, ALU.mult)
                link(s)
                if u:
                    dve.wait_ge(w_turned, u)
                for t in range(TT):
                    s = nc.vector.scalar_tensor_tensor(weights[:, t, :], probs[:, 0, t, :], inv[:, t:t + 1],
                                                       masked[:, t, :], ALU.mult, ALU.add)
                s.then_inc(weights_ready, 1)

            def norm_heads(g, first=0, last=HEADS_C):
                dve.wait_ge(head_copied, HEADS_C * g + last)
                inverse_root(head_rstd[:, TT * first:TT * last], head_ss[:, TT * first:TT * last], HD)
                for n in range(first, last):
                    for t in range(TT):
                        o = rows[:, g % 2, t, n * HD:(n + 1) * HD]
                        i = TT * n + t
                        s = nc.vector.scalar_tensor_tensor(o, o, head_rstd[:, i:i + 1], g_bo if g < B_GROUPS else g_ao,
                                                           ALU.mult, ALU.mult)
                if last == HEADS_C:
                    s.then_inc(rows_ready, 1)

            def attention_step(s):
                u, phase = divmod(s, 3)
                if phase == 1 and u < HEADS:
                    maxima(u)

            def attention_late(s):
                u, phase = divmod(s, 3)
                if phase == 1:
                    if u < HEADS:
                        finish_weights(u)
                    if u == HEADS - 1:
                        norm_heads(GROUPS - 1, 0, HEADS_C - 1)
                    if u == HEADS:
                        norm_heads(GROUPS - 1, HEADS_C - 1)
                if phase == 2 and 0 < u < HEADS and u % HEADS_C == 0:
                    norm_heads(u // HEADS_C - 1)

            def turn_mixed(s):
                g = s // 3 // HEADS_C - 1
                turn_split_lo(ROWS[R_MIX] + g, mix_hi, mix_lo, 4 * g, 0)

            for c in range(2):
                dve.wait_ge(x_landed[c], 32)
                gain_x(ROWS[R_NORM1] + c, c, 0)
            for c in range(3):
                if c == 2:
                    split_lo(IN1, 0, 8, 2, 3, PARTS_D)
                turn_split_lo(ROWS[R_NORM1] + c, h_hi, h_lo, 4 * c, xg_at[c])
                if c:
                    dve.wait_ge(x_landed[c + 1], 32)
                    gain_x(ROWS[R_NORM1] + c + 1, c + 1, c)
                if c < 2:
                    split_lo(IN1, 0, 8, c, c + 1, PARTS_D)
            split_lo(IN1, 0, 8, 3, 4, PARTS_D)
            ffn(IN1, OUT1, ROWS[R_FFN1], 0, False)
            for g in range(GROUPS):
                for j in range(SEG):
                    s = SEG * (g - 1) + j - 1
                    if s >= 0:
                        attention_step(s)
                    if turned_at(s):
                        turn_mixed(s)
                    v = 2 * (SEG * g + j) + 4
                    split_lo(QKV, 0, 0, v, v + 1, PARTS_D)
                    if s >= 0:
                        attention_late(s)
                    split_lo(QKV, 0, 0, v + 1, v + 2, PARTS_D)
                    if g == 0 and j == 1:
                        turn_split_lo(ROWS[R_NORMX] + 3, h_hi, h_lo, 12, xg_at[3])
                        norm_factor(1)
                    if j in (6, 9):
                        scale_qk(2 * g + j // 9)
                    if g == 0 and j == 10:
                        negative_lambda()
            for s, n, count in tail():
                attention_step(s - 1)
                if turned_at(s - 1):
                    turn_mixed(s - 1)
                attention_late(s - 1)
                split_lo(PROJ, 0, 0, n + 4, n + count + 4, PARTS_D)
            turn_mixed(SEG * GROUPS + 2)
            for v in range(sum(TAIL) + 4, 2 * len(PROJ_ORDER) + 4):
                split_lo(PROJ, 0, 0, v, v + 1, PARTS_D)
                if v in XG_UPDATE:
                    c = XG_UPDATE[v]
                    update_x(PROJ, c, v - 3, 1.0)
                    if c == 0:
                        dve.wait_ge(gain_landed, 32)
                    r = ROWS[R_NORM2] + c
                    gain_x(r, c, r if c == 0 else r - 1)
                if v - 4 in XG_TURN:
                    c = XG_TURN[v - 4]
                    turn_split_lo(ROWS[R_NORM2] + c, h_hi, h_lo, 4 * c, 0)
            ffn(IN2, OUT2, ROWS[R_FFN2], 2, True)

        @block.gpsimd
        def _(pool):
            chain = [0]

            def link(ins):
                chain[0] += 1
                ins.then_inc(pool_chain, 1)
                pool.wait_ge(pool_chain, chain[0])

            pool.wait_ge(const_landed, 16 * 11)
            for m in range(2 * GROUPS):
                g, kind = divmod(m, 2)
                width = SUB if g < B_GROUPS else HD
                heads, half = NC // width, width // 8
                gain = (g_bq, g_bk)[kind] if g < B_GROUPS else (g_aq, g_ak)[kind]
                cos, sin = rope[g < B_GROUPS]
                whole = qkv[:, g % 2, kind, :, :].rearrange("p t (h d) -> p (t h) d", d=width)
                pool.wait_ge(qk_scaled, m + 1)
                link(nc.gpsimd.tensor_tensor(whole, whole, gain.unsqueeze(1).to_broadcast([P, TT * heads, width]),
                                             ALU.mult))
                rows4 = qkv[:, g % 2, kind, :, :].rearrange("p t (h d) -> p t h d", d=width)
                x1, x2 = rows4[:, :, :, 0:half], rows4[:, :, :, half:2 * half]
                temps = [rot[:, n, :].rearrange("p (t h r) -> p t h r", t=TT, h=heads) for n in range(4)]
                for n, (v, f) in enumerate(((x1, cos), (x2, sin), (x2, cos), (x1, sin))):
                    s = nc.gpsimd.tensor_tensor(temps[n], v, f.unsqueeze(2).to_broadcast([P, TT, heads, half]), ALU.mult)
                link(s)
                nc.gpsimd.tensor_tensor(x1, temps[0], temps[1], ALU.subtract)
                nc.gpsimd.tensor_tensor(x2, temps[2], temps[3], ALU.add).then_inc(qk_normed, 1)


_INS = ["x", "ffn1_norm", "ffn1_w_in", "ffn1_w_out", "mix_norm", "w_in", "a_q_norm", "a_k_norm", "b_q_norm",
        "b_k_norm", "lambda_q1", "lambda_k1", "lambda_q2", "lambda_k2", "a_out_norm", "b_out_norm", "w_out",
        "ffn2_norm", "ffn2_w_in", "ffn2_w_out"]


def kernel(**inputs):
    import concourse.bacc as bacc
    from concourse.bass_utils import run_bass_kernel_spmd

    nc = bacc.Bacc("TRN2", target_bir_lowering=False, num_devices=1, dynamic_dma_scratch_size=1024)
    arrays = {f"in_{name}": np.ascontiguousarray(inputs[name]) for name in _INS}
    arrays["in_consts"] = shape_constants()
    args = [nc.dram_tensor(n, a.shape, mybir.dt.from_np(a.dtype), kind="ExternalInput").ap()
            for n, a in arrays.items()]
    out = nc.dram_tensor("out_y", (1, SEQ, D), F32, kind="ExternalOutput").ap()
    hybrid_layer_kernel(nc, *args, out)
    r = run_bass_kernel_spmd(nc, [arrays], core_ids=[0])
    return r.results[0]["out_y"]
```
